# Optimizing a Trainium2 kernel written in Bass

```python
import math
import jax, jax.numpy as jnp
from jax import lax
import numpy as np

D_MODEL = 1024
BATCH = 1
SEQ = 512
DEPTH = 2

N_A_LAYERS = DEPTH // 2
N_B_LAYERS = DEPTH - N_A_LAYERS
LRU_WIDTH = D_MODEL
LRU_BLOCKS = 8
LRU_BLOCK_W = LRU_WIDTH // LRU_BLOCKS
CONV_W = 4
LRU_C = 8.0
N_HEADS = 8
HEAD_DIM = D_MODEL // N_HEADS // 2
V_DIM = 2 * HEAD_DIM
QK_WIDTH = N_HEADS * 2 * HEAD_DIM
V_WIDTH = N_HEADS * V_DIM
D_FF = 4 * D_MODEL
Q_BLOCK = 128
NORM_EPS = 1e-6
SUBLN_EPS = 1e-5

kernel_name = "hawk_yoco_diff_attention_trunk"

def rmsnorm(x, g, eps=NORM_EPS):
    x32 = x.astype(jnp.float32)
    y = x32 * lax.rsqrt(jnp.mean(x32 * x32, axis=-1, keepdims=True) + eps)
    return (y * g.astype(jnp.float32)).astype(x.dtype)

def alibi_slopes(n_heads):
    return jnp.asarray(np.array([2.0 ** (-8.0 * (h + 1) / n_heads) for h in range(n_heads)], dtype=np.float32))

def sq_relu_mlp(h, w1, w2):
    u = jax.nn.relu(h @ w1)
    return (u * u) @ w2

def _lru_combine(c1, c2):
    a1, b1 = c1
    a2, b2 = c2
    return a1 * a2, a2 * b1 + b2

def recurrent_block(h, w_in, b_in, conv_w, conv_b, gate_w, gate_b, lam, w_out):
    B, S, _ = h.shape
    xy = h @ w_in + b_in
    xb, yb = jnp.split(xy, 2, axis=-1)
    gate = jax.nn.gelu(yb)
    xc = lax.conv_general_dilated(
        xb, conv_w[:, None, :], window_strides=(1,), padding=((CONV_W - 1, 0),),
        dimension_numbers=('NWC', 'WIO', 'NWC'), feature_group_count=LRU_WIDTH) + conv_b
    x32 = xc.astype(jnp.float32)
    xg = x32.reshape(B, S, LRU_BLOCKS, LRU_BLOCK_W)
    g = jnp.einsum('bsnc,gncd->gbsnd', xg, gate_w.astype(jnp.float32)).reshape(2, B, S, LRU_WIDTH)
    g = g + gate_b.astype(jnp.float32)[:, None, None, :]
    r = jax.nn.sigmoid(g[0])
    i = jax.nn.sigmoid(g[1])
    log_a = -LRU_C * r * jax.nn.softplus(-lam.astype(jnp.float32))
    a = jnp.exp(log_a)
    bx = jnp.sqrt(-jnp.expm1(2.0 * log_a)) * (i * x32)
    _, hs = lax.associative_scan(_lru_combine, (a, bx), axis=1)
    return (hs.astype(h.dtype) * gate) @ w_out

def diff_attention(h, w_q, lam_vecs, subln_g, w_o, k, v, slopes, lam_init):
    B, S, _ = h.shape
    nb = S // Q_BLOCK
    q = (h @ w_q).reshape(B, nb, Q_BLOCK, N_HEADS, 2, HEAD_DIM).transpose(1, 0, 2, 3, 4, 5)
    lv = lam_vecs.astype(jnp.float32)
    lam = jnp.exp(jnp.sum(lv[0] * lv[1])) - jnp.exp(jnp.sum(lv[2] * lv[3])) + lam_init
    scale = HEAD_DIM ** -0.5
    key_pos = jnp.arange(S)

    def block(args):
        qb, bi = args
        q_pos = bi * Q_BLOCK + jnp.arange(Q_BLOCK)
        rel = q_pos[:, None] - key_pos[None, :]
        bias = jnp.where(rel[None] >= 0, -slopes[:, None, None] * rel[None].astype(jnp.float32), -jnp.inf)
        s = jnp.einsum('bqhcd,bkhcd->bhcqk', qb, k).astype(jnp.float32) * scale
        p = jax.nn.softmax(s + bias[None, :, None], axis=-1)
        w = p[:, :, 0] - lam * p[:, :, 1]
        return jnp.einsum('bhqk,bkhe->bqhe', w.astype(v.dtype), v)

    o = lax.map(block, (q, jnp.arange(nb)))
    o = o.transpose(1, 0, 2, 3, 4).reshape(B, S, N_HEADS, V_DIM)
    o = rmsnorm(o, subln_g, SUBLN_EPS) * (1.0 - lam_init)
    return o.reshape(B, S, V_WIDTH) @ w_o

def setup_inputs(seed: int = 0) -> dict:
    key = jax.random.key(seed)
    ks = jax.random.split(key, 24)
    f32 = jnp.float32
    nA, nB = N_A_LAYERS, N_B_LAYERS
    res_scale = (2.0 * DEPTH) ** -0.5

    def nrm(k, shape, fan_in, extra=1.0):
        return jax.random.normal(k, shape, f32) * (fan_in ** -0.5) * extra

    def gain(k, shape):
        return 1.0 + 0.02 * jax.random.normal(k, shape, f32)

    a0 = jax.random.uniform(ks[0], (nA, LRU_WIDTH), f32, 0.9, 0.999)
    s0 = a0 ** (1.0 / LRU_C)
    a_lambda = jnp.log(s0) - jnp.log1p(-s0)
    return {
        "x": jax.random.normal(ks[1], (BATCH, SEQ, D_MODEL), f32),
        "a_norm": gain(ks[2], (nA, D_MODEL)),
        "a_w_in": nrm(ks[3], (nA, D_MODEL, 2 * LRU_WIDTH), D_MODEL),
        "a_b_in": 0.01 * jax.random.normal(ks[4], (nA, 2 * LRU_WIDTH), f32),
        "a_conv_w": nrm(ks[5], (nA, CONV_W, LRU_WIDTH), CONV_W),
        "a_conv_b": 0.01 * jax.random.normal(ks[6], (nA, LRU_WIDTH), f32),
        "a_gate_w": nrm(ks[7], (nA, 2, LRU_BLOCKS, LRU_BLOCK_W, LRU_BLOCK_W), LRU_BLOCK_W),
        "a_gate_b": 0.01 * jax.random.normal(ks[8], (nA, 2, LRU_WIDTH), f32),
        "a_lambda": a_lambda,
        "a_w_out": nrm(ks[9], (nA, LRU_WIDTH, D_MODEL), LRU_WIDTH, res_scale),
        "kv_norm": gain(ks[10], (D_MODEL,)),
        "w_kv": nrm(ks[11], (D_MODEL, QK_WIDTH + V_WIDTH), D_MODEL),
        "b_norm": gain(ks[12], (nB, D_MODEL)),
        "b_w_q": nrm(ks[13], (nB, D_MODEL, QK_WIDTH), D_MODEL),
        "b_lam": 0.1 * jax.random.normal(ks[14], (nB, 4, HEAD_DIM), f32),
        "b_subln": gain(ks[15], (nB, V_DIM)),
        "b_w_o": nrm(ks[16], (nB, V_WIDTH, D_MODEL), V_WIDTH, res_scale),
        "mlp_norm": gain(ks[17], (DEPTH, D_MODEL)),
        "mlp_w1": nrm(ks[18], (DEPTH, D_MODEL, D_FF), D_MODEL),
        "mlp_w2": nrm(ks[19], (DEPTH, D_FF, D_MODEL), D_FF, res_scale),
        "final_norm": gain(ks[20], (D_MODEL,)),
    }

def reference(x, a_norm, a_w_in, a_b_in, a_conv_w, a_conv_b, a_gate_w, a_gate_b, a_lambda, a_w_out,
              kv_norm, w_kv, b_norm, b_w_q, b_lam, b_subln, b_w_o,
              mlp_norm, mlp_w1, mlp_w2, final_norm):
    B, S, _ = x.shape
    slopes = alibi_slopes(N_HEADS)
    k = None
    v = None
    for l in range(DEPTH):
        if l < N_A_LAYERS:
            x = x + recurrent_block(rmsnorm(x, a_norm[l]), a_w_in[l], a_b_in[l], a_conv_w[l], a_conv_b[l],
                                    a_gate_w[l], a_gate_b[l], a_lambda[l], a_w_out[l])
        else:
            j = l - N_A_LAYERS
            lam_init = 0.8 - 0.6 * math.exp(-0.3 * l)
            x = x + diff_attention(rmsnorm(x, b_norm[j]), b_w_q[j], b_lam[j], b_subln[j], b_w_o[j],
                                   k, v, slopes, lam_init)
        x = x + sq_relu_mlp(rmsnorm(x, mlp_norm[l]), mlp_w1[l], mlp_w2[l])
        if l == N_A_LAYERS - 1:
            kv = rmsnorm(x, kv_norm) @ w_kv
            k = kv[..., :QK_WIDTH].reshape(B, S, N_HEADS, 2, HEAD_DIM)
            v = kv[..., QK_WIDTH:].reshape(B, S, N_HEADS, V_DIM)
    return rmsnorm(x, final_norm)


_drawn_inputs = setup_inputs


def setup_inputs(seed=0):
    import zlib

    import numpy as np

    out = dict(_drawn_inputs(seed))
    spreads = {}
    factors = {'a_norm': 8.0,
     'a_b_in': 3.252,
     'a_conv_b': 3.303,
     'a_gate_b': 8.0,
     'kv_norm': 26.019,
     'b_norm': 25.632,
     'b_subln': 64.0,
     'mlp_norm': 10.268,
     'final_norm': 8.734,
     'b_lam': 4.408}
    for name, (base, spread) in spreads.items():
        noise = np.random.default_rng([zlib.crc32(name.encode()), seed]).standard_normal(out[name].shape)
        drawn = base * np.exp(spread * noise) if base else spread * noise
        out[name] = __import__('jax').numpy.asarray(drawn.astype(out[name].dtype))
    for name, factor in factors.items():
        out[name] = (out[name] * factor).astype(out[name].dtype)
    return out
```

```python
import math
from contextlib import ExitStack

import numpy as np

import concourse.bass as bass
from concourse import mybir

P = 128
D = 1024
S = 512
NCH = D // P
HEADS = 8
HEAD_DIM = D // HEADS // 2
V_DIM = 2 * HEAD_DIM
D_FF = 4 * D
GROUPS = D_FF // D
CONV_W = 4
TILE = NCH * P
QB = S // P
NORM_EPS = 1e-6
SUBLN_EPS = 1e-5
LRU_C = 8.0
LAM_INIT = 0.8 - 0.6 * math.exp(-0.3)
GELU_C = math.sqrt(2.0 / math.pi)
GELU_CUBIC = 0.044715
SLOPE_0 = 2.0 ** (-8.0 / HEADS)
MASKED = 3.0e38

T_XB = 0
T_YB = T_XB + NCH
T_OUT = T_YB + NCH
T_MLP0 = T_OUT + NCH
T_V = T_MLP0 + 2 * NCH * GROUPS
T_KQ = T_V + NCH
T_O = T_KQ + 2 * HEADS
T_MLP1 = T_O + NCH
TILES = T_MLP1 + 2 * NCH * GROUPS

O_A = 0
O_Y = O_A + NCH
O_M0 = O_Y + NCH
O_U0 = O_M0 + NCH
O_KV = O_U0 + NCH * GROUPS
O_Q = O_KV + NCH
O_ATT = O_Q + NCH
O_M1 = O_ATT + NCH
O_U1 = O_M1 + NCH

N_A, N_M0, N_KV, N_M1, N_FINAL = range(5)

COLS = {}
_at = 0
for _name, _n in (("a_norm", NCH), ("b_in", 2 * NCH), ("conv_w", CONV_W * NCH), ("conv_b", NCH),
                  ("gate_b", 2 * NCH), ("lambda", NCH), ("kv_norm", NCH), ("b_norm", NCH),
                  ("mlp_norm", 2 * NCH), ("final_norm", NCH), ("subln", 1)):
    COLS[_name] = _at
    _at += _n
NCOLS = _at

BANK_GATE_R, BANK_GATE_I, BANK_COLS, BANK_STATS = 4, 5, 6, 7
BANK_SCORES, BANK_T, BANK_O = 2, 6, 7
RING = 4
RAWS = 2


def at(first, i, per):
    return first if i is None else i * per + first


def build(nc, x_t, weights, gate_weights, vectors, lam_vecs, out_t):
    F32 = mybir.dt.float32
    F32R = mybir.dt.float32r
    ACT = mybir.ActivationFunctionType
    ALU = mybir.AluOpType

    keep = ExitStack()
    with keep:
        def sb(name, shape, dt, stack=keep):
            return stack.enter_context(nc.sbuf_tensor(name, shape, dt))

        def sem(name):
            return keep.enter_context(nc.semaphore(name))

        x = sb("x", [P, NCH, S], F32)
        w_raw = sb("w_raw", [P, RAWS, TILE], F32)
        w_hi = sb("w_hi", [P, RING, TILE], F32R)
        w_lo = sb("w_lo", [P, RING, TILE], F32R)
        h_hi = sb("h_hi", [P, NCH, S], F32R)
        h_lo = sb("h_lo", [P, NCH, S], F32R)
        u_hi = sb("u_hi", [P, NCH, S], F32R)
        u_lo = sb("u_lo", [P, NCH, S], F32R)
        work = sb("work", [P, 4, S], F32)
        acc = sb("acc", [P, S], F32)
        rstd = sb("rstd", [P, S], F32)
        vec = sb("vec", [P, NCOLS], F32)
        small = sb("small", [P, 10, NCH], F32)
        cols = sb("cols", [P, 3, QB], F32)
        rstd_col = sb("rstd_col", [P, QB], F32)
        ones = sb("ones", [P, P], F32)
        three_halves = sb("three_halves", [P, S], F32)
        absorb = sb("absorb", [P, 2], F32)

        lru = ExitStack()
        lru_r = sb("lru_r", [P, NCH, S], F32, lru)
        lru_v = sb("lru_v", [P, NCH, S], F32, lru)
        lru_x = sb("lru_x", [P, NCH, S], F32, lru)
        gelu = sb("gelu", [P, NCH, S], F32, lru)
        xc_hi = sb("xc_hi", [P, S], F32R, lru)
        xc_lo = sb("xc_lo", [P, S], F32R, lru)
        lru.close()
        flat_v = lru_v[:, :, :].rearrange("p c s -> p (c s)")
        zr = [flat_v[:, (1 + i) * S:(2 + i) * S] for i in range(2)]
        PAD = CONV_W - 1
        xb_pad = [flat_v[:, 3 * S + i * (S + PAD):3 * S + (i + 1) * (S + PAD)] for i in range(2)]
        xc = [lru_v[:, 6 + i, :] for i in range(2)]
        GW = 2 * NCH * P
        gw_raw = gelu[:, :, :].rearrange("p c s -> p (c s)")[:, 0:GW]
        gw_hi = u_hi[:, :, :].rearrange("p c s -> p (c s)")[:, 0:GW]
        gw_lo = u_lo[:, :, :].rearrange("p c s -> p (c s)")[:, 0:GW]

        value = sb("value", [P, QB, D], F32)
        att = sb("att", [P, HEADS, S], F32)
        prob = sb("prob", [P, 2, 2, S], F32)
        prob_t = sb("prob_t", [P, QB, S], F32)
        kq = sb("kq", [P, 2, 2, S], F32)
        value_h = sb("value_h", [P, 2, QB, P], F32)
        bias = sb("bias", [P, S], F32)
        o_raw = sb("o_raw", [P, S], F32)
        sub = sb("sub", [P, 3, S], F32)
        ident = sb("ident", [P, P], F32)
        lam_in = sb("lam_in", [P, 4 * HEAD_DIM], F32)
        lam_tmp = sb("lam_tmp", [P, HEAD_DIM], F32)
        lam_s = sb("lam_s", [P, 8], F32)
        neg_min = sb("neg_min", [P, 2, 2], F32)
        total = sb("total", [P, 2, 2], F32)
        inv = sb("inv", [P, 2, 2], F32)
        inv_lam = sb("inv_lam", [P, 2], F32)

        ps = keep.enter_context(nc.psum_tensor("ps", [P, 8, S], F32))

        x_in = [sem(f"x_in{i}") for i in range(4)]
        vec_in = sem("vec_in")
        gw_in = sem("gw_in")
        lam_loaded = sem("lam_loaded")
        raw_in = [sem(f"raw_in{i}") for i in range(RAWS)]
        whi_done = sem("whi_done")
        wlo_done = sem("wlo_done")
        tile_done = sem("tile_done")
        bank_read = sem("bank_read")
        ohi_done = sem("ohi_done")
        olo_done = sem("olo_done")
        sq_done = sem("sq_done")
        acc_done = sem("acc_done")
        stats_done = sem("stats_done")
        guess_done = sem("guess_done")
        rstd_done = sem("rstd_done")
        consts_done = sem("consts_done")
        xb_done = sem("xb_done")
        conv_done = sem("conv_done")
        xchi_done = sem("xchi_done")
        xclo_done = sem("xclo_done")
        gwhi_done = sem("gwhi_done")
        gwlo_done = sem("gwlo_done")
        gates_mm = sem("gates_mm")
        gates_act = sem("gates_act")
        ix_done = sem("ix_done")
        decay_done = sem("decay_done")
        sq_u_done = sem("sq_u_done")
        y_done = sem("y_done")
        ysq_done = sem("ysq_done")
        arg_done = sem("arg_done")
        tanh_done = sem("tanh_done")
        lru_exp = sem("lru_exp")
        lru_q = sem("lru_q")
        lru_a = sem("lru_a")
        sqrt_done = sem("sqrt_done")
        bx_done = sem("bx_done")
        hs_done = sem("hs_done")
        lam_prod = sem("lam_prod")
        lam_exp = sem("lam_exp")
        scores_mm = sem("scores_mm")
        scores_read = sem("scores_read")
        exp_done = sem("exp_done")
        prob_done = sem("prob_done")
        trans_mm = sem("trans_mm")
        trans_read = sem("trans_read")
        value_done = sem("value_done")
        att_mm = sem("att_mm")
        att_read = sem("att_read")
        sub_mm = sem("sub_mm")
        sub_read = sem("sub_read")
        sub_guess = sem("sub_guess")
        sub_rstd = sem("sub_rstd")
        att_done = sem("att_done")
        y_out = sem("y_out")
        stored = sem("stored")
        act_own = sem("act_own")
        dve_own = sem("dve_own")
        pool_own = sem("pool_own")

        def col(name, n=0):
            c = COLS[name] + n
            return vec[:, c:c + 1]

        class Own:

            def __init__(self, eng, s):
                self.eng, self.s, self.n, self.i, self.per = eng, s, 0, None, 0

            def step(self, ins):
                ins.then_inc(self.s, 1)
                self.n += 1

            def wait(self):
                self.eng.wait_ge(self.s, at(self.n, self.i, self.per))

            def enter(self, i, per):
                self.i, self.per, self.first = i, per, self.n

            def leave(self, times):
                assert self.n == self.first + self.per, (self.n, self.first, self.per)
                self.i, self.n = None, self.first + self.per * times

        block = keep.enter_context(nc.Block())

        @block.sync
        def _(sp):
            def load(t, slot):
                sp.dma_start(w_raw[:, slot, :], weights[t]).then_inc(raw_in[slot], 16)

            sp.dma_start(vec[:, :], vectors).then_inc(vec_in, 16)
            for t in range(RAWS):
                load(t, t)
            with sp.Fori(1, TILES // RAWS) as i:
                for slot in range(RAWS):
                    sp.wait_ge(wlo_done, i * RAWS + (slot - RAWS + 1))
                    sp.dma_start(w_raw[:, slot, :],
                                 weights[bass.ds(i * RAWS + slot, 1)].rearrange("o p f -> (o p) f")
                                 ).then_inc(raw_in[slot], 16)
            for m in range(NCH):
                sp.wait_ge(y_out, m + 1)
                sp.dma_start(out_t[m], att[:, m, :]).then_inc(stored, 16)
            sp.wait_ge(stored, 16 * NCH)

        @block.gpsimd
        def _(pool):
            own = Own(pool, pool_own)
            own.step(nc.gpsimd.memset(ones[:, :], 1.0))
            own.step(nc.gpsimd.memset(three_halves[:, :], 1.5))
            for i in range(2):
                own.step(nc.gpsimd.memset(xb_pad[i][:, 0:PAD], 0.0))
            own.wait()
            nc.gpsimd.memset(cols[:, 0, 0:1], 0.0).then_inc(consts_done, 1)

            def accumulate(n):
                for m in range(NCH):
                    pool.wait_ge(sq_done, n * NCH + m + 1)
                    if n * NCH + m:
                        pool.wait_ge(acc_done, n * NCH + m)
                    if m == 0:
                        nc.gpsimd.tensor_copy(acc[:, :], work[:, 0, :]).then_inc(acc_done, 1)
                    else:
                        nc.gpsimd.tensor_tensor(acc[:, :], acc[:, :], work[:, m % 2, :],
                                                ALU.add).then_inc(acc_done, 1)

            def newton(v, guess, guess_sq, result, done):
                own.step(nc.gpsimd.tensor_tensor(guess_sq, guess_sq, v, ALU.mult))
                own.wait()
                n = guess_sq.shape[1]
                own.step(nc.gpsimd.tensor_tensor(guess_sq, three_halves[:, 0:n], guess_sq,
                                                 ALU.subtract))
                own.wait()
                nc.gpsimd.tensor_tensor(result, guess, guess_sq, ALU.mult).then_inc(done, 1)

            def norm(n):
                accumulate(n)
                pool.wait_ge(guess_done, n + 1)
                newton(work[:, 2, :], work[:, 3, :], work[:, 1, :], rstd[:, :], rstd_done)

            norm(N_A)
            for m in range(NCH):
                g = work[:, 2 + m % 2, :]
                pool.wait_ge(ysq_done, m + 1)
                own.step(nc.gpsimd.tensor_scalar(g, g, GELU_CUBIC * GELU_C, GELU_C, ALU.mult, ALU.add))
                own.wait()
                nc.gpsimd.tensor_tensor(g, g, gelu[:, m, :], ALU.mult).then_inc(arg_done, 1)
                if m < NCH // 2:
                    for c in (2 * m, 2 * m + 1):
                        pool.wait_ge(lru_q, c + 1)
                        nc.gpsimd.tensor_scalar(lru_r[:, c, :], lru_r[:, c, :], -1.0, 1.0,
                                                ALU.mult, ALU.add).then_inc(lru_a, 1)
                else:
                    for c in (2 * m - NCH, 2 * m - NCH + 1):
                        pool.wait_ge(sqrt_done, c + 1)
                        nc.gpsimd.tensor_tensor(lru_x[:, c, :], lru_x[:, c, :], lru_v[:, c, :],
                                                ALU.mult).then_inc(bx_done, 1)
            norm(N_M0)
            own.step(nc.gpsimd.memset(ident[:, :], 0.0))
            own.step(nc.gpsimd.iota(bias[:, :], pattern=[[-1, S]], base=S - P, channel_multiplier=1,
                                    allow_small_or_imprecise_dtypes=True))
            own.wait()
            nc.gpsimd.affine_select(out=ident[:, :], in_=ident[:, :], compare_op=ALU.not_equal,
                                    fill=1.0, base=0, pattern=[[-1, P]],
                                    channel_multiplier=1).then_inc(consts_done, 1)
            own.step(nc.gpsimd.affine_select(out=bias[:, :], in_=bias[:, :], compare_op=ALU.is_ge,
                                             fill=MASKED, base=S - P, pattern=[[-1, S]],
                                             channel_multiplier=1))
            own.wait()
            nc.gpsimd.tensor_scalar(bias[:, :], bias[:, :], SLOPE_0, 0.0, ALU.mult,
                                    ALU.add).then_inc(consts_done, 1)

            accumulate(N_KV)
            pool.wait_ge(guess_done, N_KV + 1)
            newton(work[:, 2, :], work[:, 3, :], work[:, 1, :], rstd[:, :], rstd_done)
            newton(cols[:, 0, :], cols[:, 1, :], cols[:, 2, :], rstd_col[:, :], rstd_done)

            def head_values(h, i, p):
                if i is not None or h >= 2:
                    pool.wait_ge(att_mm, at(h - 1, i, 2))
                src = value[:, :, h * P:(h + 1) * P] if i is None else \
                    value[:, :, bass.ds(i * (2 * P) + h * P, P)]
                nc.gpsimd.tensor_copy(value_h[:, p, :, :], src).then_inc(value_done, 1)

            def sub_newton(h, i):
                pool.wait_ge(sub_guess, at(h + 1, i, 2))
                newton(sub[:, 0, :], sub[:, 1, :], sub[:, 2, :], sub[:, 2, :], sub_rstd)

            pool.wait_ge(bank_read, T_KQ)
            head_values(0, None, 0)
            head_values(1, None, 1)
            with pool.Fori(0, (HEADS - 2) // 2) as i:
                own.enter(i, 4)
                for k in range(2):
                    head_values(2 + k, i, k)
                    sub_newton(k, i)
                own.leave((HEADS - 2) // 2)
            sub_newton(HEADS - 2, None)
            sub_newton(HEADS - 1, None)
            norm(N_M1)
            norm(N_FINAL)

        @block.scalar
        def _(act):
            own = Own(act, act_own)
            for j in range(4):
                nc.scalar.dma_start(x[:, 2 * j:2 * j + 2, :],
                                    x_t[2 * j:2 * j + 2].rearrange("c p s -> p c s")
                                    ).then_inc(x_in[j], 16)
            nc.scalar.dma_start(gw_raw, gate_weights).then_inc(gw_in, 16)
            nc.scalar.dma_start(lam_in[:, :], lam_vecs).then_inc(lam_loaded, 16)

            def split_hi(t, i=None, per=0):
                if i is None and t >= TILES:
                    return
                act.wait_ge(raw_in[t % RAWS], at(16 * (t // RAWS + 1), i, 16 * per // RAWS))
                if i is not None or t >= RING:
                    act.wait_ge(tile_done, at(t - RING + 1, i, per))
                nc.scalar.activation(w_hi[:, t % RING, :], w_raw[:, t % RAWS, :],
                                     ACT.Copy).then_inc(whi_done, 1)

            def operand_hi(dst, m, gain):
                nc.scalar.activation(dst[:, m, :], x[:, m, :], ACT.Copy,
                                     scale=gain).then_inc(ohi_done, 1)

            def square(n, m):
                k = n * NCH + m
                if k >= 2:
                    act.wait_ge(acc_done, k - 1)
                nc.scalar.activation(work[:, m % 2, :], x[:, m, :], ACT.Square).then_inc(sq_done, 1)

            def guess(v, g, g_sq, psum, scale, eps, read, done):
                ins = nc.scalar.activation(v, psum, ACT.Copy, scale=scale / 2, bias=eps / 2)
                if read is None:
                    own.step(ins)
                    own.wait()
                else:
                    ins.then_inc(read[0], 1)
                    act.wait_ge(read[0], read[1])
                own.step(nc.scalar.activation(g, v, ACT.Ln, scale=2.0))
                own.wait()
                own.step(nc.scalar.activation(g, g, ACT.Exp, scale=-0.5))
                own.wait()
                ins = nc.scalar.activation(g_sq, g, ACT.Square)
                if done is not None:
                    ins.then_inc(done, 1)

            def norm_guess(n):
                act.wait_ge(stats_done, n + 1)
                if n == N_KV:
                    guess(cols[:, 0, :], cols[:, 1, :], cols[:, 2, :], ps[:, BANK_COLS, 0:QB],
                          1.0 / D, NORM_EPS, None, None)
                guess(work[:, 2, :], work[:, 3, :], work[:, 1, :], ps[:, BANK_STATS, :],
                      1.0 / D, NORM_EPS, None, guess_done)

            nc.scalar.preload_act_table_set("natural_log_exp_and_others")
            act.wait_ge(decay_done, 1)
            nc.scalar.activation(small[:, 1, :], small[:, 0, :], ACT.Exp, scale=-1.0).then_inc(decay_done, 1)
            act.wait_ge(vec_in, 16)
            for m in range(NCH):
                act.wait_ge(x_in[m // 2], 16)
                operand_hi(h_hi, m, col("a_norm", m))
                square(N_A, m)
                if m < RING:
                    split_hi(m)
            norm_guess(N_A)

            def xb_bias(m):
                act.wait_ge(bank_read, T_XB + m + 1)
                if m >= 2:
                    act.wait_ge(conv_done, m - 1)
                if m == 0:
                    act.wait_ge(consts_done, 1)
                nc.scalar.activation(xb_pad[m % 2][:, PAD:], zr[m % 2], ACT.Identity,
                                     bias=col("b_in", m)).then_inc(xb_done, 1)

            def gate_sigmoids(m):
                act.wait_ge(gates_mm, m + 1)
                nc.scalar.activation(lru_r[:, m, :], ps[:, BANK_GATE_R, :], ACT.Sigmoid,
                                     bias=col("gate_b", m))
                nc.scalar.activation(lru_x[:, m, :], ps[:, BANK_GATE_I, :], ACT.Sigmoid,
                                     bias=col("gate_b", NCH + m)).then_inc(gates_act, 1)

            for m in range(NCH):
                xb_bias(m)
                if m == 0:
                    act.wait_ge(gw_in, 16)
                    nc.scalar.activation(gw_hi, gw_raw, ACT.Copy).then_inc(gwhi_done, 1)
                if m:
                    gate_sigmoids(m - 1)
                act.wait_ge(conv_done, m + 1)
                if m:
                    act.wait_ge(gates_mm, m)
                nc.scalar.activation(xc_hi[:, :], xc[m % 2], ACT.Copy).then_inc(xchi_done, 1)
                split_hi(T_XB + m + RING)

            for m in range(NCH):
                act.wait_ge(bank_read, T_YB + m + 1)
                if m == 0:
                    act.wait_ge(gwlo_done, 1)
                nc.scalar.activation(gelu[:, m, :], work[:, m % 2, :], ACT.Identity,
                                     bias=col("b_in", NCH + m)).then_inc(y_done, 1)
                act.wait_ge(y_done, m + 1)
                nc.scalar.activation(work[:, 2 + m % 2, :], gelu[:, m, :],
                                     ACT.Square).then_inc(ysq_done, 1)
                if m == 0:
                    gate_sigmoids(NCH - 1)
                    act.wait_ge(ix_done, NCH)
                if m < NCH // 2:
                    for c in (2 * m, 2 * m + 1):
                        if m == 0 and c == 0:
                            act.wait_ge(decay_done, 3)
                            act.wait_ge(gates_act, NCH)
                        own.step(nc.scalar.activation(lru_v[:, c, :], lru_r[:, c, :], ACT.Tanh,
                                                      scale=small[:, 8, c:c + 1]))
                        own.wait()
                        nc.scalar.activation(lru_r[:, c, :], lru_r[:, c, :], ACT.Exp,
                                             scale=small[:, 9, c:c + 1]).then_inc(lru_exp, 1)
                act.wait_ge(arg_done, m + 1)
                nc.scalar.activation(work[:, 2 + m % 2, :], work[:, 2 + m % 2, :],
                                     ACT.Tanh).then_inc(tanh_done, 1)
                if m == NCH // 2:
                    for c in range(NCH):
                        act.wait_ge(lru_q, c + 1)
                        nc.scalar.activation(lru_v[:, c, :], lru_v[:, c, :], ACT.Sqrt,
                                             scale=-1.0).then_inc(sqrt_done, 1)
                if m >= NCH // 2:
                    for c in (2 * m - NCH, 2 * m - NCH + 1):
                        act.wait_ge(hs_done, c + 1)
                        nc.scalar.activation(u_hi[:, c, :], lru_v[:, c, :],
                                             ACT.Copy).then_inc(ohi_done, 1)
                split_hi(T_YB + m + RING)
            nc.scalar.preload_act_table_set("natural_log_exp_and_others")

            def residual_step(t, n, gains):
                for m in range(NCH):
                    act.wait_ge(bank_read, t + m + 1)
                    if gains is not None:
                        operand_hi(h_hi, m, col(gains[0], gains[1] + m))
                    square(n, m)
                    split_hi(t + m + RING)

            residual_step(T_OUT, N_M0, ("mlp_norm", 0))

            def mlp_up(t0, o0, i):
                per = 2 * NCH
                for m in range(NCH):
                    act.wait_ge(bank_read, at(t0 + m + 1, i, per))
                    nc.scalar.activation(work[:, 2 + m % 2, :], work[:, m % 2, :],
                                         ACT.Square).then_inc(sq_u_done, 1)
                    act.wait_ge(sq_u_done, at(o0 + m + 1, i, NCH))
                    nc.scalar.activation(u_hi[:, m, :], work[:, 2 + m % 2, :],
                                         ACT.Copy).then_inc(ohi_done, 1)
                    split_hi(t0 + m + RING, i, per)

            def mlp(layer, t0, n_stats, n, gains):
                first_u = layer * NCH * GROUPS
                norm_guess(n_stats)
                with act.Fori(0, GROUPS - 1) as i:
                    mlp_up(t0, first_u, i)
                    for m in range(NCH):
                        split_hi(t0 + NCH + m + RING, i, 2 * NCH)
                last = GROUPS - 1
                mlp_up(t0 + last * 2 * NCH, first_u + last * NCH, None)
                residual_step(t0 + last * 2 * NCH + NCH, n, gains)

            mlp(0, T_MLP0, N_M0, N_KV, ("kv_norm", 0))

            act.wait_ge(lam_prod, 2)
            nc.scalar.activation(lam_s[:, 2:4], lam_s[:, 0:2], ACT.Exp).then_inc(lam_exp, 1)
            for m in range(NCH):
                operand_hi(u_hi, m, col("b_norm", m))
                if m == 0:
                    norm_guess(N_KV)
                split_hi(T_V + m + RING)
            for t in (T_KQ, T_KQ + 1):
                split_hi(t + RING)

            def exps(h, i, j):
                a = QB * h + j
                n = (QB - j) * P
                act.wait_ge(scores_read, at(2 * a + 2, i, 4 * QB))
                for c in range(2):
                    ins = nc.scalar.activation(prob[:, j % 2, c, 0:n], prob[:, j % 2, c, 0:n], ACT.Exp,
                                               scale=-1.0, bias=neg_min[:, j % 2, c:c + 1],
                                               accum_out=total[:, j % 2, c:c + 1])
                ins.then_inc(exp_done, 1)

            def transposed(h, i, j):
                a = QB * h + j
                qb = QB - 1 - j
                act.wait_ge(trans_mm, at(a + 1, i, 2 * QB))
                if j == 0 and (i is not None or h > 0):
                    act.wait_ge(att_mm, at(h, i, 2))
                nc.scalar.activation(
                    prob_t[:, 0:qb + 1, qb * P:(qb + 1) * P],
                    ps[:, BANK_T, 0:(qb + 1) * P].rearrange("p (b q) -> p b q", q=P),
                    ACT.Copy).then_inc(trans_read, 1)

            def att_out(h, i):
                act.wait_ge(att_mm, at(h + 1, i, 2))
                if i is not None or h > 0:
                    act.wait_ge(att_done, at(h, i, 2))
                nc.scalar.activation(o_raw[:, :], ps[:, BANK_O, :], ACT.Copy)
                nc.scalar.activation(sub[:, 0, :], ps[:, BANK_O, :], ACT.Square).then_inc(att_read, 1)

            def sub_guess_of(h, i):
                act.wait_ge(sub_mm, at(h + 1, i, 2))
                guess(sub[:, 0, :], sub[:, 1, :], sub[:, 2, :], ps[:, BANK_O, :], 1.0 / V_DIM,
                      SUBLN_EPS, (sub_read, at(h + 1, i, 2)), sub_guess)

            def head(h, i, first=False, last=False):
                t = T_KQ + 2 * h + 2
                if not first:
                    att_out(h - 1, i)
                exps(h, i, 0)
                exps(h, i, 1)
                if not first:
                    sub_guess_of(h - 1, i)
                exps(h, i, 2)
                transposed(h, i, 0)
                if not last:
                    split_hi(t + RING, i, 4)
                exps(h, i, 3)
                for j in range(1, QB):
                    transposed(h, i, j)
                if not last:
                    split_hi(t + 1 + RING, i, 4)

            head(0, None, first=True)
            with act.Fori(0, (HEADS - 2) // 2) as i:
                own.enter(i, 4)
                head(1, i)
                head(2, i)
                own.leave((HEADS - 2) // 2)
            head(HEADS - 1, None, last=True)
            att_out(HEADS - 1, None)
            sub_guess_of(HEADS - 1, None)
            for m in range(HEADS):
                act.wait_ge(att_done, m + 1)
                nc.scalar.activation(u_hi[:, m, :], att[:, m, :], ACT.Copy).then_inc(ohi_done, 1)
            residual_step(T_O, N_M1, ("mlp_norm", NCH))
            mlp(1, T_MLP1, N_M1, N_FINAL, None)
            norm_guess(N_FINAL)

        @block.vector
        def _(dve):
            own = Own(dve, dve_own)

            def split_lo(t, i=None, per=0):
                if i is None and t >= TILES:
                    return
                dve.wait_ge(whi_done, at(t + 1, i, per))
                nc.vector.tensor_tensor(w_lo[:, t % RING, :], w_raw[:, t % RAWS, :],
                                        w_hi[:, t % RING, :], ALU.subtract).then_inc(wlo_done, 1)

            def operand_lo(dst_lo, dst_hi, m, gain, o):
                dve.wait_ge(ohi_done, o + 1)
                nc.vector.scalar_tensor_tensor(out=dst_lo[:, m, :], in0=x[:, m, :], scalar=gain,
                                               in1=dst_hi[:, m, :], op0=ALU.mult,
                                               op1=ALU.subtract).then_inc(olo_done, 1)

            dve.wait_ge(vec_in, 16)
            lam = vec[:, COLS["lambda"]:COLS["lambda"] + NCH]
            own.step(nc.vector.tensor_scalar(small[:, 7, :], lam, -1.0, None, ALU.mult))
            own.wait()
            nc.vector.tensor_tensor(small[:, 0, :], lam, small[:, 7, :], ALU.max).then_inc(decay_done, 1)
            dve.wait_ge(decay_done, 2)
            own.step(nc.vector.tensor_scalar(small[:, 2, :], small[:, 1, :], 2.0, None, ALU.add))
            own.wait()
            own.step(nc.vector.reciprocal(small[:, 3, :], small[:, 2, :]))
            own.wait()
            own.step(nc.vector.tensor_tensor(small[:, 4, :], small[:, 1, :], small[:, 3, :], ALU.mult))
            own.wait()
            own.step(nc.vector.tensor_tensor(small[:, 5, :], small[:, 4, :], small[:, 4, :], ALU.mult))
            own.wait()
            own.step(nc.vector.tensor_scalar(small[:, 6, :], small[:, 5, :], 1.0 / 17.0, None, ALU.mult))
            own.wait()
            for k in range(15, 1, -2):
                own.step(nc.vector.scalar_tensor_tensor(
                    out=small[:, 6, :], in0=small[:, 6, :], scalar=1.0 / k, in1=small[:, 5, :],
                    op0=ALU.add, op1=ALU.mult))
                own.wait()
            own.step(nc.vector.scalar_tensor_tensor(
                out=small[:, 6, :], in0=small[:, 6, :], scalar=1.0, in1=small[:, 4, :],
                op0=ALU.add, op1=ALU.mult))
            own.step(nc.vector.tensor_scalar(small[:, 7, :], small[:, 7, :], 0.0, None, ALU.max))
            own.wait()
            own.step(nc.vector.scalar_tensor_tensor(
                out=small[:, 7, :], in0=small[:, 6, :], scalar=2.0, in1=small[:, 7, :],
                op0=ALU.mult, op1=ALU.add))
            own.wait()
            own.step(nc.vector.tensor_scalar(small[:, 8, :], small[:, 7, :], LRU_C / 2, None, ALU.mult))
            nc.vector.tensor_scalar(small[:, 9, :], small[:, 7, :], -LRU_C, None,
                                    ALU.mult).then_inc(decay_done, 1)

            for m in range(NCH):
                dve.wait_ge(x_in[m // 2], 16)
                operand_lo(h_lo, h_hi, m, col("a_norm", m), O_A + m)
                if m < RING - 1:
                    split_lo(m)

            def gated_input(m):
                dve.wait_ge(gates_act, m + 1)
                nc.vector.scalar_tensor_tensor(out=lru_x[:, m, :], in0=lru_x[:, m, :], scalar=0.5,
                                               in1=xc[m % 2], op0=ALU.mult,
                                               op1=ALU.mult).then_inc(ix_done, 1)

            dve.wait_ge(rstd_done, N_A + 1)
            for m in range(NCH):
                t = T_XB + m
                dve.wait_ge(tile_done, t + 1)
                if m >= 2:
                    dve.wait_ge(xb_done, m - 1)
                nc.vector.tensor_tensor(zr[m % 2], ps[:, t % RING, :], rstd[:, :],
                                        ALU.mult).then_inc(bank_read, 1)
                split_lo(t + RING - 1)
                if m == 0:
                    dve.wait_ge(gwhi_done, 1)
                    nc.vector.tensor_tensor(gw_lo, gw_raw, gw_hi, ALU.subtract).then_inc(gwlo_done, 1)
                dve.wait_ge(xb_done, m + 1)
                if m >= 2:
                    dve.wait_ge(ix_done, m - 1)
                pad = xb_pad[m % 2]
                own.step(nc.vector.tensor_scalar(xc[m % 2], pad[:, PAD:PAD + S],
                                                 col("conv_w", PAD * NCH + m), col("conv_b", m),
                                                 ALU.mult, ALU.add))
                for j in range(PAD - 1, -1, -1):
                    own.wait()
                    ins = nc.vector.scalar_tensor_tensor(
                        out=xc[m % 2], in0=pad[:, j:j + S], scalar=col("conv_w", j * NCH + m),
                        in1=xc[m % 2], op0=ALU.mult, op1=ALU.add)
                    if j:
                        own.step(ins)
                    else:
                        ins.then_inc(conv_done, 1)
                if m:
                    gated_input(m - 1)
                dve.wait_ge(xchi_done, m + 1)
                nc.vector.tensor_tensor(xc_lo[:, :], xc[m % 2], xc_hi[:, :],
                                        ALU.subtract).then_inc(xclo_done, 1)

            for m in range(NCH):
                t = T_YB + m
                dve.wait_ge(tile_done, t + 1)
                if m >= 2:
                    dve.wait_ge(y_done, m - 1)
                nc.vector.tensor_tensor(work[:, m % 2, :], ps[:, t % RING, :], rstd[:, :],
                                        ALU.mult).then_inc(bank_read, 1)
                if m == 0:
                    gated_input(NCH - 1)
                split_lo(t + RING - 1)
                if m < NCH // 2:
                    for c in (2 * m, 2 * m + 1):
                        dve.wait_ge(lru_exp, c + 1)
                        own.step(nc.vector.scalar_tensor_tensor(
                            out=lru_r[:, c, :], in0=lru_r[:, c, :], scalar=1.0, in1=lru_v[:, c, :],
                            op0=ALU.add, op1=ALU.mult))
                        own.wait()
                        nc.vector.scalar_tensor_tensor(
                            out=lru_v[:, c, :], in0=lru_r[:, c, :], scalar=-2.0, in1=lru_r[:, c, :],
                            op0=ALU.add, op1=ALU.mult).then_inc(lru_q, 1)
                dve.wait_ge(tanh_done, m + 1)
                own.step(nc.vector.scalar_tensor_tensor(
                    out=gelu[:, m, :], in0=work[:, 2 + m % 2, :], scalar=1.0, in1=gelu[:, m, :],
                    op0=ALU.add, op1=ALU.mult))
                if m >= NCH // 2:
                    own.wait()
                    for c in (2 * m - NCH, 2 * m - NCH + 1):
                        dve.wait_ge(bx_done, c + 1)
                        dve.wait_ge(lru_a, c + 1)
                        own.step(nc.vector.tensor_tensor_scan(
                            lru_v[:, c, :], lru_r[:, c, :], lru_x[:, c, :], 0.0, ALU.mult, ALU.add))
                        own.wait()
                        nc.vector.tensor_tensor(lru_v[:, c, :], lru_v[:, c, :], gelu[:, c, :],
                                                ALU.mult).then_inc(hs_done, 1)
                    for c in (2 * m - NCH, 2 * m - NCH + 1):
                        dve.wait_ge(ohi_done, O_Y + c + 1)
                        nc.vector.tensor_tensor(u_lo[:, c, :], lru_v[:, c, :], u_hi[:, c, :],
                                                ALU.subtract).then_inc(olo_done, 1)

            def residual_step(t, o0, gains):
                for m in range(NCH):
                    dve.wait_ge(tile_done, t + m + 1)
                    nc.vector.tensor_tensor(x[:, m, :], x[:, m, :], ps[:, (t + m) % RING, :],
                                            ALU.add).then_inc(bank_read, 1)
                    split_lo(t + m + RING - 1)
                    if gains is not None:
                        operand_lo(h_lo, h_hi, m, col(gains[0], gains[1] + m), o0 + m)

            residual_step(T_OUT, O_M0, ("mlp_norm", 0))

            def mlp_up(t0, u0, o0, i):
                per = 2 * NCH
                for m in range(NCH):
                    t = t0 + m
                    dve.wait_ge(tile_done, at(t + 1, i, per))
                    if i is not None or u0 + m >= 2:
                        if i is not None and u0 + m < 2:
                            pass
                        else:
                            dve.wait_ge(sq_u_done, at(u0 + m - 1, i, NCH))
                    nc.vector.scalar_tensor_tensor(
                        out=work[:, m % 2, :], in0=ps[:, t % RING, :], scalar=0.0, in1=rstd[:, :],
                        op0=ALU.max, op1=ALU.mult).then_inc(bank_read, 1)
                    split_lo(t + RING - 1, i, per)
                    dve.wait_ge(ohi_done, at(o0 + m + 1, i, NCH))
                    nc.vector.tensor_tensor(u_lo[:, m, :], work[:, 2 + m % 2, :], u_hi[:, m, :],
                                            ALU.subtract).then_inc(olo_done, 1)

            def mlp(layer, t0, n_stats, o_next, gains):
                u0 = layer * NCH * GROUPS
                o0 = O_U1 if layer else O_U0
                dve.wait_ge(rstd_done, n_stats + 1 + (n_stats > N_KV))
                with dve.Fori(0, GROUPS - 1) as i:
                    mlp_up(t0, u0, o0, i)
                    for m in range(NCH):
                        t = t0 + NCH + m
                        dve.wait_ge(tile_done, at(t + 1, i, 2 * NCH))
                        nc.vector.tensor_tensor(x[:, m, :], x[:, m, :], ps[:, t % RING, :],
                                                ALU.add).then_inc(bank_read, 1)
                        split_lo(t + RING - 1, i, 2 * NCH)
                last = GROUPS - 1
                mlp_up(t0 + last * 2 * NCH, u0 + last * NCH, o0 + last * NCH, None)
                residual_step(t0 + last * 2 * NCH + NCH, o_next, gains)

            mlp(0, T_MLP0, N_M0, O_KV, ("kv_norm", 0))

            dve.wait_ge(lam_loaded, 16)
            for k in range(2):
                nc.vector.tensor_tensor_reduce(
                    out=lam_tmp[:, :], in0=lam_in[:, 2 * k * HEAD_DIM:(2 * k + 1) * HEAD_DIM],
                    in1=lam_in[:, (2 * k + 1) * HEAD_DIM:(2 * k + 2) * HEAD_DIM], scale=1.0, scalar=0.0,
                    op0=ALU.mult, op1=ALU.add, accum_out=lam_s[:, k:k + 1]).then_inc(lam_prod, 1)
                dve.wait_ge(lam_prod, k + 1)
            dve.wait_ge(lam_exp, 1)
            own.step(nc.vector.tensor_tensor(lam_s[:, 4:5], lam_s[:, 3:4], lam_s[:, 2:3], ALU.subtract))
            own.wait()
            own.step(nc.vector.tensor_scalar(lam_s[:, 5:6], lam_s[:, 4:5], LAM_INIT, None, ALU.subtract))
            own.step(nc.vector.tensor_scalar(lam_s[:, 6:7], col("subln"), 1.0 - LAM_INIT, None, ALU.mult))
            own.wait()
            neg_lam, sub_gain = lam_s[:, 5:6], lam_s[:, 6:7]

            for half in range(2):
                for s in range(4):
                    m = half * 4 + s
                    if s == 3:
                        dve.wait_ge(tile_done, T_V + m + 1)
                        if half == 0:
                            dve.wait_ge(rstd_done, N_KV + 2)
                        for tok in range(QB):
                            nc.vector.tensor_scalar(value[:, tok, half * S:(half + 1) * S],
                                                    ps[:, tok, :], rstd_col[:, tok:tok + 1], None,
                                                    ALU.mult).then_inc(bank_read, 1)
                    split_lo(T_V + m + RING - 1)
                    operand_lo(u_lo, u_hi, m, col("b_norm", m), O_Q + m)

            def key(h, i):
                t = T_KQ + 2 * h
                dve.wait_ge(tile_done, at(t + 1, i, 4))
                nc.vector.tensor_tensor(kq[:, h % 2, 0, :], ps[:, 0, :], rstd[:, :],
                                        ALU.mult).then_inc(bank_read, 1)
                split_lo(t + RING - 1, i, 4)

            def query(h, i):
                t = T_KQ + 2 * h + 1
                dve.wait_ge(tile_done, at(t + 1, i, 4))
                nc.vector.scalar_tensor_tensor(out=kq[:, h % 2, 1, :], in0=ps[:, 1, :],
                                               scalar=-HEAD_DIM ** -0.5, in1=rstd[:, :], op0=ALU.mult,
                                               op1=ALU.mult).then_inc(bank_read, 1)
                split_lo(t + RING - 1, i, 4)

            def biased(h, i, j):
                a = QB * h + j
                n = (QB - j) * P
                dve.wait_ge(scores_mm, at(a + 1, i, 2 * QB))
                if i is not None or a >= 2:
                    dve.wait_ge(trans_mm, at(a - 1, i, 2 * QB))
                nc.vector.memset(absorb[:, j % 2:j % 2 + 1], 0.0)
                for c in range(2):
                    nc.vector.tensor_tensor_reduce(
                        out=prob[:, j % 2, c, 0:n], in0=ps[:, BANK_SCORES + 2 * (j % 2) + c, 0:n],
                        in1=bias[:, S - n:S], scale=1.0, scalar=MASKED, op0=ALU.add, op1=ALU.min,
                        accum_out=neg_min[:, j % 2, c:c + 1]).then_inc(scores_read, 1)

            def combined(h, i, j):
                a = QB * h + j
                n = (QB - j) * P
                s = j % 2
                dve.wait_ge(exp_done, at(a + 1, i, 2 * QB))
                own.step(nc.vector.reciprocal(inv[:, s, :], total[:, s, :]))
                own.wait()
                own.step(nc.vector.tensor_tensor(inv_lam[:, s:s + 1], inv[:, s, 1:2], neg_lam, ALU.mult))
                own.wait()
                own.step(nc.vector.tensor_scalar(prob[:, s, 1, 0:n], prob[:, s, 1, 0:n],
                                                 inv_lam[:, s:s + 1], None, ALU.mult))
                own.wait()
                nc.vector.scalar_tensor_tensor(out=prob[:, s, 0, 0:n], in0=prob[:, s, 0, 0:n],
                                               scalar=inv[:, s, 0:1], in1=prob[:, s, 1, 0:n],
                                               op0=ALU.mult, op1=ALU.add).then_inc(prob_done, 1)

            def normed(h, i):
                dve.wait_ge(sub_rstd, at(h + 1, i, 2))
                dst = att[:, h, :] if i is None else \
                    att[:, bass.ds(i * 2 + h, 1), :].rearrange("p o s -> p (o s)")
                nc.vector.scalar_tensor_tensor(out=dst, in0=o_raw[:, :], scalar=sub_gain,
                                               in1=sub[:, 2, :], op0=ALU.mult,
                                               op1=ALU.mult).then_inc(att_done, 1)

            OWN_PER_HEAD = 3 * QB + 1

            def head(h, i, first=False, last=False):
                biased(h, i, 0)
                biased(h, i, 1)
                combined(h, i, 0)
                biased(h, i, 2)
                combined(h, i, 1)
                if not last:
                    key(h + 1, i)
                biased(h, i, 3)
                dve.wait_ge(scores_read, at(2 * QB * (h + 1), i, 4 * QB))
                own.step(nc.vector.tensor_scalar(bias[:, :], bias[:, :], 0.5, None, ALU.mult))
                combined(h, i, 2)
                combined(h, i, 3)
                if not last:
                    query(h + 1, i)
                if not first:
                    normed(h - 1, i)

            dve.wait_ge(rstd_done, N_KV + 2)
            key(0, None)
            query(0, None)
            dve.wait_ge(consts_done, 3)
            head(0, None, first=True)
            with dve.Fori(0, (HEADS - 2) // 2) as i:
                own.enter(i, 2 * OWN_PER_HEAD)
                head(1, i)
                head(2, i)
                own.leave((HEADS - 2) // 2)
            head(HEADS - 1, None, last=True)
            for m in range(HEADS):
                if m == HEADS - 1:
                    normed(HEADS - 1, None)
                dve.wait_ge(ohi_done, O_ATT + m + 1)
                nc.vector.tensor_tensor(u_lo[:, m, :], att[:, m, :], u_hi[:, m, :],
                                        ALU.subtract).then_inc(olo_done, 1)
            residual_step(T_O, O_M1, ("mlp_norm", NCH))
            mlp(1, T_MLP1, N_M1, None, None)
            dve.wait_ge(rstd_done, N_FINAL + 2)
            for m in range(NCH):
                nc.vector.scalar_tensor_tensor(out=att[:, m, :], in0=x[:, m, :],
                                               scalar=col("final_norm", m), in1=rstd[:, :],
                                               op0=ALU.mult, op1=ALU.mult).then_inc(y_out, 1)

        @block.tensor
        def _(pe):
            def passes(bank, slot, hi, lo, k, parts=(0, 1, 2)):
                ws = slice(k * P, (k + 1) * P)
                pairs = ((w_hi, hi), (w_hi, lo), (w_lo, hi))
                for n in parts:
                    w, o = pairs[n]
                    ins = nc.tensor.matmul(ps[:, bank, :], w[:, slot, ws], o[:, k, :],
                                           start=(k == 0 and n == 0), stop=(k == NCH - 1 and n == 2))
                return ins

            def tile_starts(t, free, i=None, per=0):
                pe.wait_ge(wlo_done, at(t + 1, i, per))
                if i is not None or free > 0:
                    pe.wait_ge(bank_read, at(free, i, per))

            def tile(t, hi, lo, o=None, i=None, per=0, o_per=0):
                tile_starts(t, t - RING + 1, i, per)
                for k in range(NCH):
                    if o is not None:
                        pe.wait_ge(olo_done, at(o + k + 1, i, o_per))
                    ins = passes(t % RING, t % RING, hi, lo, k)
                ins.then_inc(tile_done, 1)

            def stats(n):
                pe.wait_ge(acc_done, (n + 1) * NCH)
                ins = nc.tensor.matmul(ps[:, BANK_STATS, :], ones[:, :], acc[:, :], start=True, stop=True)
                if n == N_KV:
                    for tok in range(QB):
                        ins = nc.tensor.matmul(ps[:, BANK_COLS, tok:tok + 1],
                                               acc[:, tok * P:(tok + 1) * P], ones[:, 0:1],
                                               start=True, stop=True)
                ins.then_inc(stats_done, 1)

            def gates(m):
                pe.wait_ge(xclo_done, m + 1)
                if m == 0:
                    pe.wait_ge(gwlo_done, 1)
                else:
                    pe.wait_ge(gates_act, m)
                for g, bank in ((0, BANK_GATE_R), (1, BANK_GATE_I)):
                    ws = slice((g * NCH + m) * P, (g * NCH + m + 1) * P)
                    for n, (w, o) in enumerate(((gw_hi, xc_hi), (gw_hi, xc_lo), (gw_lo, xc_hi))):
                        ins = nc.tensor.matmul(ps[:, bank, :], w[:, ws], o[:, :],
                                               start=(n == 0), stop=(n == 2))
                ins.then_inc(gates_mm, 1)

            pe.wait_ge(consts_done, 1)
            for m in range(NCH):
                tile(T_XB + m, h_hi, h_lo, O_A if m == 0 else None)
                if m == 0:
                    stats(N_A)
                else:
                    gates(m - 1)
            for m in range(NCH):
                tile(T_YB + m, h_hi, h_lo)
                if m == 0:
                    gates(NCH - 1)
            for m in range(NCH):
                tile(T_OUT + m, u_hi, u_lo, O_Y if m == 0 else None)

            def mlp(t0, o_h, o_u, n):
                per = 2 * NCH
                for k in range(NCH):
                    pe.wait_ge(olo_done, o_h + k + 1)
                stats(n)

                def group(first_t, first_o, i):
                    for m in range(NCH):
                        tile(first_t + m, h_hi, h_lo, None, i, per)
                    for m in range(NCH):
                        tile(first_t + NCH + m, u_hi, u_lo, first_o if m == 0 else None, i, per, NCH)

                with pe.Fori(0, GROUPS - 1) as i:
                    group(t0, o_u, i)
                last = GROUPS - 1
                group(t0 + last * per, o_u + last * NCH, None)

            mlp(T_MLP0, O_M0, O_U0, N_M0)

            for half in range(2):
                for s in range(4):
                    t = T_V + half * 4 + s
                    tile_starts(t, T_V + 4 * half)
                    for kk in range(2):
                        k = 2 * s + kk
                        if half == 0:
                            pe.wait_ge(olo_done, O_KV + k + 1)
                        cs = slice(kk * S, (kk + 1) * S)
                        for tok in range(QB):
                            ts = slice(tok * P, (tok + 1) * P)
                            for n, (o, w) in enumerate(((h_hi, w_hi), (h_lo, w_hi), (h_hi, w_lo))):
                                ins = nc.tensor.matmul(ps[:, tok, :], o[:, k, ts], w[:, t % RING, cs],
                                                       start=(k == 0 and n == 0),
                                                       stop=(k == NCH - 1 and n == 2))
                    ins.then_inc(tile_done, 1)
                    if half == 0 and s == 0:
                        stats(N_KV)

            def kq_part(h, i, part):
                which, quarter = divmod(part, 4)
                t = T_KQ + 2 * h + which
                if quarter == 0:
                    tile_starts(t, max(t - 1, T_KQ), i, 4)
                for k in (2 * quarter, 2 * quarter + 1):
                    if which == 0:
                        ins = passes(0, t % RING, h_hi, h_lo, k)
                    else:
                        ins = passes(1, t % RING, u_hi, u_lo, k)
                if quarter == 3:
                    ins.then_inc(tile_done, 1)

            def scores(h, i, j):
                a = QB * h + j
                qb = QB - 1 - j
                n = (qb + 1) * P
                if j == 0:
                    pe.wait_ge(bank_read, at(T_KQ + 2 * h + 2, i, 4))
                if i is not None or a >= 2:
                    pe.wait_ge(scores_read, at(2 * (a - 1), i, 4 * QB))
                for c in range(2):
                    rows = slice(c * HEAD_DIM, (c + 1) * HEAD_DIM)
                    ins = nc.tensor.matmul(ps[:, BANK_SCORES + 2 * (j % 2) + c, 0:n],
                                           kq[rows, h % 2, 1, qb * P:(qb + 1) * P],
                                           kq[rows, h % 2, 0, 0:n], start=True, stop=True)
                ins.then_inc(scores_mm, 1)

            def transposes(h, i, j):
                a = QB * h + j
                qb = QB - 1 - j
                pe.wait_ge(prob_done, at(a + 1, i, 2 * QB))
                if i is not None or a >= 1:
                    pe.wait_ge(trans_read, at(a, i, 2 * QB))
                for kb in range(qb + 1):
                    ks = slice(kb * P, (kb + 1) * P)
                    ins = nc.tensor.transpose(ps[:, BANK_T, ks], prob[:, j % 2, 0, ks], ident[:, :])
                ins.then_inc(trans_mm, 1)

            def attend(h, i):
                pe.wait_ge(trans_read, at(QB * (h + 1), i, 2 * QB))
                pe.wait_ge(value_done, at(h + 1, i, 2))
                if i is not None or h > 0:
                    pe.wait_ge(sub_read, at(h, i, 2))
                for kb in range(QB):
                    ins = nc.tensor.matmul(ps[:, BANK_O, kb * P:S], value_h[:, h % 2, kb, :],
                                           prob_t[:, kb, kb * P:S], start=(kb == 0),
                                           stop=(kb == QB - 1), skip_group_check=True)
                ins.then_inc(att_mm, 1)

            def sub_sum(h, i):
                pe.wait_ge(att_read, at(h + 1, i, 2))
                nc.tensor.matmul(ps[:, BANK_O, :], ones[:, :], sub[:, 0, :], start=True,
                                 stop=True).then_inc(sub_mm, 1)

            def head(h, i, first=False, last=False):
                def part(n):
                    if not last:
                        kq_part(h + 1, i, n)

                scores(h, i, 0)
                scores(h, i, 1)
                part(0)
                part(1)
                if not first:
                    sub_sum(h - 1, i)
                scores(h, i, 2)
                part(2)
                transposes(h, i, 0)
                part(3)
                scores(h, i, 3)
                part(4)
                transposes(h, i, 1)
                part(5)
                transposes(h, i, 2)
                part(6)
                transposes(h, i, 3)
                part(7)
                attend(h, i)

            for k in range(NCH):
                pe.wait_ge(olo_done, O_Q + k + 1)
            for part in range(8):
                kq_part(0, None, part)
            pe.wait_ge(consts_done, 3)
            head(0, None, first=True)
            with pe.Fori(0, (HEADS - 2) // 2) as i:
                head(1, i)
                head(2, i)
            head(HEADS - 1, None, last=True)
            sub_sum(HEADS - 1, None)

            for m in range(NCH):
                tile(T_O + m, u_hi, u_lo, O_ATT if m == 0 else None)
            mlp(T_MLP1, O_M1, O_U1, N_M1)
            stats(N_FINAL)


def kernel(**inputs):
    import concourse.bacc as bacc
    from concourse.bass_utils import run_bass_kernel_spmd

    a = {k: np.asarray(v) for k, v in inputs.items()}

    def by_output(w):
        n = w.shape[1] // P
        return w.reshape(NCH, P, n, P).transpose(2, 1, 0, 3).reshape(n, P, TILE)

    def by_input(w):
        return w.reshape(4, 2, P, S).transpose(0, 2, 1, 3).reshape(4, P, TILE)

    def mlp(layer):
        for g in range(GROUPS):
            yield by_output(a["mlp_w1"][layer][:, g * D:(g + 1) * D])
            yield by_output(a["mlp_w2"][layer][g * D:(g + 1) * D])

    keys, queries = by_output(a["w_kv"][:, :D]), by_output(a["b_w_q"][0])
    parts = [by_output(a["a_w_in"][0]), by_output(a["a_w_out"][0]), *mlp(0)]
    parts += [by_input(a["w_kv"][:, D + h * S:D + (h + 1) * S]) for h in range(2)]
    parts += [np.stack([keys, queries], axis=1).reshape(2 * HEADS, P, TILE)]
    parts += [by_output(a["b_w_o"][0]), *mlp(1)]
    weights = np.ascontiguousarray(np.concatenate(parts))

    def columns(v):
        return np.asarray(v).reshape(-1, P).T

    vectors = np.ascontiguousarray(np.concatenate([columns(a[n]) for n in (
        "a_norm", "a_b_in", "a_conv_w", "a_conv_b", "a_gate_b", "a_lambda", "kv_norm", "b_norm",
        "mlp_norm", "final_norm", "b_subln")], axis=1))
    arrays = {
        "x_t": np.ascontiguousarray(a["x"][0].T).reshape(NCH, P, S),
        "weights": weights,
        "gate_weights": np.ascontiguousarray(
            a["a_gate_w"][0].transpose(2, 0, 1, 3).reshape(P, 2 * NCH * P)),
        "vectors": vectors,
        "lam_vecs": np.ascontiguousarray(np.broadcast_to(a["b_lam"].reshape(1, -1), (P, 4 * HEAD_DIM))),
    }
    nc = bacc.Bacc("TRN2", target_bir_lowering=False, num_devices=1)
    f32 = mybir.dt.float32
    args = [nc.dram_tensor(n, v.shape, f32, kind="ExternalInput").ap() for n, v in arrays.items()]
    out = nc.dram_tensor("y_t", [NCH, P, S], f32, kind="ExternalOutput").ap()
    build(nc, *args, out)
    r = run_bass_kernel_spmd(nc, [arrays], core_ids=[0])
    y = r.results[0]["y_t"].reshape(D, S).T
    return np.ascontiguousarray(y).reshape(1, S, D)
```

```python
import math
from contextlib import ExitStack

import numpy as np

import concourse.bass as bass
from concourse import mybir

P = 128
D = 1024
S = 512
NCH = D // P
HEADS = 8
HEAD_DIM = D // HEADS // 2
V_DIM = 2 * HEAD_DIM
D_FF = 4 * D
GROUPS = D_FF // D
CONV_W = 4
TILE = NCH * P
QB = S // P
NORM_EPS = 1e-6
SUBLN_EPS = 1e-5
LRU_C = 8.0
LAM_INIT = 0.8 - 0.6 * math.exp(-0.3)
GELU_C = math.sqrt(2.0 / math.pi)
GELU_CUBIC = 0.044715
SLOPE_0 = 2.0 ** (-8.0 / HEADS)
MASKED = 3.0e38

T_XB = 0
T_YB = T_XB + NCH
T_OUT = T_YB + NCH
T_MLP0 = T_OUT + NCH
T_V = T_MLP0 + 2 * NCH * GROUPS
T_KQ = T_V + NCH
T_O = T_KQ + 2 * HEADS
T_MLP1 = T_O + NCH
TILES = T_MLP1 + 2 * NCH * GROUPS

O_A = 0
O_Y = O_A + NCH
O_M0 = O_Y + NCH
O_U0 = O_M0 + NCH
O_KV = O_U0 + NCH * GROUPS
O_Q = O_KV + NCH
O_ATT = O_Q + NCH
O_M1 = O_ATT + NCH
O_U1 = O_M1 + NCH

N_A, N_M0, N_KV, N_M1, N_FINAL = range(5)

COLS = {}
_at = 0
for _name, _n in (("a_norm", NCH), ("b_in", 2 * NCH), ("conv_w", CONV_W * NCH), ("conv_b", NCH),
                  ("gate_b", 2 * NCH), ("lambda", NCH), ("kv_norm", NCH), ("b_norm", NCH),
                  ("mlp_norm", 2 * NCH), ("final_norm", NCH), ("subln", 1)):
    COLS[_name] = _at
    _at += _n
NCOLS = _at

BANK_COLS, BANK_STATS = 6, 7
BANK_GATES = ((4, 5), (6, 7))
BANK_SCORES, BANK_T, BANK_O = 2, 6, 7
RING = 4
XC = 4
WARM_UP = 4
RAWS = 2
OPEN = 3
POOL_LO = range(RING, T_OUT)
DECAY_AT = {0: range(0, 4), 1: range(4, 8)}
SQRT_AT = 1
SCAN_AT = {2: (0, 1), 3: (2, 3), 4: (4, 5), 5: (6, 7)}
GATED_AT = {2: (0, 1), 3: (2, 3), 4: (4,), 5: (5,), 6: (6,), 7: (7,)}
SPLIT_AT = {2: T_OUT + 1, 3: T_OUT + 2, 6: T_OUT + 3}
POOL_OUT = (2, 5)
DVE_OUT = (0, 1, 3, 4, 6, 7)


def at(first, i, per):
    return first if i is None else i * per + first


def build(nc, x_t, weights, gate_weights, vectors, lam_vecs, out_t):
    F32 = mybir.dt.float32
    F32R = mybir.dt.float32r
    ACT = mybir.ActivationFunctionType
    ALU = mybir.AluOpType

    keep = ExitStack()
    with keep:
        def sb(name, shape, dt, stack=keep):
            return stack.enter_context(nc.sbuf_tensor(name, shape, dt))

        def sem(name):
            return keep.enter_context(nc.semaphore(name))

        x = sb("x", [P, NCH, S], F32)
        w_raw = sb("w_raw", [P, RAWS, TILE], F32)
        w_hi = sb("w_hi", [P, RING, TILE], F32R)
        w_lo = sb("w_lo", [P, RING, TILE], F32R)
        h_hi = sb("h_hi", [P, NCH, S], F32R)
        h_lo = sb("h_lo", [P, NCH, S], F32R)
        u_hi = sb("u_hi", [P, NCH, S], F32R)
        u_lo = sb("u_lo", [P, NCH, S], F32R)
        work = sb("work", [P, 4, S], F32)
        acc = sb("acc", [P, S], F32)
        rstd = sb("rstd", [P, S], F32)
        vec = sb("vec", [P, NCOLS], F32)
        small = sb("small", [P, 10, NCH], F32)
        cols = sb("cols", [P, 3, QB], F32)
        eps_col = sb("eps_col", [P, 1], F32)
        rstd_col = sb("rstd_col", [P, QB], F32)
        ones = sb("ones", [P, P], F32)
        three_halves = sb("three_halves", [P, S], F32)
        absorb = sb("absorb", [P, 2], F32)

        lru = ExitStack()
        lru_r = sb("lru_r", [P, NCH, S], F32, lru)
        lru_v = sb("lru_v", [P, NCH, S], F32, lru)
        lru_x = sb("lru_x", [P, NCH, S], F32, lru)
        gelu = sb("gelu", [P, NCH, S], F32, lru)
        lru.close()
        flat_v = lru_v[:, :, :].rearrange("p c s -> p (c s)")
        zr = [flat_v[:, (1 + i) * S:(2 + i) * S] for i in range(2)]
        PAD = CONV_W - 1
        xb_pad = [flat_v[:, 3 * S + i * (S + PAD):3 * S + (i + 1) * (S + PAD)] for i in range(2)]
        GW = 2 * NCH * P
        gw_raw = gelu[:, :, :].rearrange("p c s -> p (c s)")[:, 0:GW]
        gw_hi = u_hi[:, :, :].rearrange("p c s -> p (c s)")[:, 0:GW]
        gw_lo = u_lo[:, :, :].rearrange("p c s -> p (c s)")[:, 0:GW]
        xc = [lru_v[:, 6, :], lru_v[:, 7, :], gelu[:, GW // S, :], gelu[:, GW // S + 1, :]]
        xc_hi = [u_hi[:, GW // S + i, :] for i in range(2)]
        xc_lo = [u_lo[:, GW // S + i, :] for i in range(2)]

        value = sb("value", [P, QB, D], F32)
        att = sb("att", [P, HEADS, S], F32)
        prob = sb("prob", [P, 2, 2, S], F32)
        prob_t = sb("prob_t", [P, QB, S], F32)
        kq = sb("kq", [P, 2, 2, S], F32)
        value_h = sb("value_h", [P, 2, QB, P], F32)
        bias = sb("bias", [P, S], F32)
        o_raw = sb("o_raw", [P, S], F32)
        sub = sb("sub", [P, 3, S], F32)
        ident = sb("ident", [P, P], F32)
        lam_in = sb("lam_in", [P, 4 * HEAD_DIM], F32)
        lam_tmp = sb("lam_tmp", [P, HEAD_DIM], F32)
        lam_s = sb("lam_s", [P, 8], F32)
        neg_min = sb("neg_min", [P, 2, 2], F32)
        total = sb("total", [P, 2, 2], F32)
        inv = sb("inv", [P, 2, 2], F32)
        inv_lam = sb("inv_lam", [P, 2], F32)

        ps = keep.enter_context(nc.psum_tensor("ps", [P, 8, S], F32))

        x_in = [sem(f"x_in{i}") for i in range(NCH)]
        vec_in = sem("vec_in")
        gw_in = sem("gw_in")
        lam_loaded = sem("lam_loaded")
        raw_in = [sem(f"raw_in{i}") for i in range(RAWS)]
        whi_done = sem("whi_done")
        wlo_done = sem("wlo_done")
        tile_done = sem("tile_done")
        bank_read = sem("bank_read")
        ohi_done = sem("ohi_done")
        olo_done = sem("olo_done")
        sq_done = sem("sq_done")
        acc_done = sem("acc_done")
        stats_done = sem("stats_done")
        ln_done = sem("ln_done")
        guess_done = sem("guess_done")
        rstd_done = sem("rstd_done")
        consts_done = sem("consts_done")
        xb_done = sem("xb_done")
        conv_done = sem("conv_done")
        xchi_done = sem("xchi_done")
        xclo_done = sem("xclo_done")
        gwhi_done = sem("gwhi_done")
        gwlo_done = sem("gwlo_done")
        gates_mm = sem("gates_mm")
        gates_act = sem("gates_act")
        ix_done = sem("ix_done")
        decay_done = sem("decay_done")
        sq_u_done = sem("sq_u_done")
        y_done = sem("y_done")
        ysq_done = sem("ysq_done")
        arg_done = sem("arg_done")
        tanh_done = sem("tanh_done")
        gelu_done = sem("gelu_done")
        lru_exp = sem("lru_exp")
        lru_q = sem("lru_q")
        lru_a = sem("lru_a")
        sqrt_done = sem("sqrt_done")
        bx_done = sem("bx_done")
        hs_done = sem("hs_done")
        lam_prod = sem("lam_prod")
        lam_exp = sem("lam_exp")
        scores_mm = sem("scores_mm")
        scores_read = sem("scores_read")
        exp_done = sem("exp_done")
        prob_done = sem("prob_done")
        trans_mm = sem("trans_mm")
        trans_read = sem("trans_read")
        value_done = sem("value_done")
        att_mm = sem("att_mm")
        att_read = sem("att_read")
        sub_mm = sem("sub_mm")
        sub_read = sem("sub_read")
        sub_guess = sem("sub_guess")
        sub_rstd = sem("sub_rstd")
        att_done = sem("att_done")
        gained = sem("gained")
        out_dve = sem("out_dve")
        out_pool = sem("out_pool")
        stored = sem("stored")
        act_own = sem("act_own")
        dve_own = sem("dve_own")
        pool_own = sem("pool_own")

        def col(name, n=0):
            c = COLS[name] + n
            return vec[:, c:c + 1]

        class Own:

            def __init__(self, eng, s):
                self.eng, self.s, self.n, self.i, self.per = eng, s, 0, None, 0

            def step(self, ins):
                ins.then_inc(self.s, 1)
                self.n += 1

            def wait(self):
                self.eng.wait_ge(self.s, at(self.n, self.i, self.per))

            def enter(self, i, per):
                self.i, self.per, self.first = i, per, self.n

            def leave(self, times):
                assert self.n == self.first + self.per, (self.n, self.first, self.per)
                self.i, self.n = None, self.first + self.per * times

        block = keep.enter_context(nc.Block())

        @block.sync
        def _(sp):
            def load(t, slot):
                sp.dma_start(w_raw[:, slot, :], weights[t]).then_inc(raw_in[slot], 16)

            sp.dma_start(vec[:, :], vectors).then_inc(vec_in, 16)
            for m in range(NCH):
                sp.dma_start(x[:, m, :], x_t[m]).then_inc(x_in[m], 16)
                if m < RAWS:
                    load(m, m)
            with sp.Fori(1, TILES // RAWS) as i:
                for slot in range(RAWS):
                    sp.wait_ge(wlo_done, i * RAWS + (slot - RAWS + 1))
                    sp.dma_start(w_raw[:, slot, :],
                                 weights[bass.ds(i * RAWS + slot, 1)].rearrange("o p f -> (o p) f")
                                 ).then_inc(raw_in[slot], 16)
            for m in range(NCH):
                if m in POOL_OUT:
                    sp.wait_ge(out_pool, POOL_OUT.index(m) + 1)
                else:
                    sp.wait_ge(out_dve, DVE_OUT.index(m) + 1)
                sp.dma_start(out_t[m], att[:, m, :]).then_inc(stored, 16)
            sp.wait_ge(stored, 16 * NCH)

        @block.gpsimd
        def _(pool):
            own = Own(pool, pool_own)
            own.step(nc.gpsimd.memset(ones[:, :], 1.0))
            own.step(nc.gpsimd.memset(three_halves[:, :], 1.5))
            own.step(nc.gpsimd.memset(eps_col[:, :], NORM_EPS))
            for i in range(2):
                own.step(nc.gpsimd.memset(xb_pad[i][:, 0:PAD], 0.0))
            own.wait()
            nc.gpsimd.memset(cols[:, 0, 0:1], 0.0).then_inc(consts_done, 1)

            def accumulate(n, chunks=NCH):
                for m in range(chunks):
                    pool.wait_ge(sq_done, n * NCH + m + 1)
                    if n * NCH + m:
                        pool.wait_ge(acc_done, n * NCH + m)
                    if m == 0:
                        nc.gpsimd.tensor_copy(acc[:, :], work[:, 0, :]).then_inc(acc_done, 1)
                    else:
                        nc.gpsimd.tensor_tensor(acc[:, :], acc[:, :], work[:, m % 2, :],
                                                ALU.add).then_inc(acc_done, 1)

            def newton(v, guess, guess_sq, result, done):
                own.step(nc.gpsimd.tensor_tensor(guess_sq, guess_sq, v, ALU.mult))
                own.wait()
                n = guess_sq.shape[1]
                own.step(nc.gpsimd.tensor_tensor(guess_sq, three_halves[:, 0:n], guess_sq,
                                                 ALU.subtract))
                own.wait()
                nc.gpsimd.tensor_tensor(result, guess, guess_sq, ALU.mult).then_inc(done, 1)

            def split_lo(t):
                pool.wait_ge(whi_done, t + 1)
                nc.gpsimd.tensor_tensor(w_lo[:, t % RING, :], w_raw[:, t % RAWS, :],
                                        w_hi[:, t % RING, :], ALU.subtract).then_inc(wlo_done, 1)

            def gated_input(m):
                pool.wait_ge(gates_act, m + 1)
                nc.gpsimd.tensor_tensor(lru_x[:, m, :], lru_x[:, m, :], xc[m % XC],
                                        ALU.mult).then_inc(ix_done, 1)

            accumulate(N_A)
            pool.wait_ge(wlo_done, POOL_LO[0])
            pool.wait_ge(gwhi_done, 1)
            nc.gpsimd.tensor_tensor(gw_lo, gw_raw, gw_hi, ALU.subtract).then_inc(gwlo_done, 1)
            for m in range(NCH):
                split_lo(m + RING)
                if m:
                    gated_input(m - 1)
            gated_input(NCH - 1)
            for c in range(NCH):
                if c in (0, 4, 6):
                    split_lo(T_YB + RING + (0, 4, 6).index(c))
                pool.wait_ge(lru_q, c + 1)
                nc.gpsimd.tensor_scalar(lru_r[:, c, :], lru_r[:, c, :], -1.0, 1.0,
                                        ALU.mult, ALU.add).then_inc(lru_a, 1)
            split_lo(T_OUT - 1)
            for c in range(NCH):
                pool.wait_ge(sqrt_done, c + 1)
                nc.gpsimd.tensor_tensor(lru_x[:, c, :], lru_x[:, c, :], lru_v[:, c, :],
                                        ALU.mult).then_inc(bx_done, 1)
            for c in range(NCH - 1):
                pool.wait_ge(ohi_done, O_Y + c + 1)
                nc.gpsimd.tensor_tensor(u_lo[:, c, :], lru_v[:, c, :], u_hi[:, c, :],
                                        ALU.subtract).then_inc(olo_done, 1)
            accumulate(N_M0)
            own.step(nc.gpsimd.memset(ident[:, :], 0.0))
            own.step(nc.gpsimd.iota(bias[:, :], pattern=[[-1, S]], base=S - P, channel_multiplier=1,
                                    allow_small_or_imprecise_dtypes=True))
            own.wait()
            nc.gpsimd.affine_select(out=ident[:, :], in_=ident[:, :], compare_op=ALU.not_equal,
                                    fill=1.0, base=0, pattern=[[-1, P]],
                                    channel_multiplier=1).then_inc(consts_done, 1)
            own.step(nc.gpsimd.affine_select(out=bias[:, :], in_=bias[:, :], compare_op=ALU.is_ge,
                                             fill=MASKED, base=S - P, pattern=[[-1, S]],
                                             channel_multiplier=1))
            own.wait()
            nc.gpsimd.tensor_scalar(bias[:, :], bias[:, :], SLOPE_0, 0.0, ALU.mult,
                                    ALU.add).then_inc(consts_done, 1)

            accumulate(N_KV)

            def head_values(h, i, p):
                if i is not None or h >= 2:
                    pool.wait_ge(att_mm, at(h - 1, i, 2))
                src = value[:, :, h * P:(h + 1) * P] if i is None else \
                    value[:, :, bass.ds(i * (2 * P) + h * P, P)]
                nc.gpsimd.tensor_copy(value_h[:, p, :, :], src).then_inc(value_done, 1)

            def sub_newton(h, i):
                pool.wait_ge(sub_guess, at(h + 1, i, 2))
                newton(sub[:, 0, :], sub[:, 1, :], sub[:, 2, :], sub[:, 2, :], sub_rstd)

            pool.wait_ge(bank_read, T_KQ)
            head_values(0, None, 0)
            head_values(1, None, 1)
            with pool.Fori(0, (HEADS - 2) // 2) as i:
                own.enter(i, 4)
                for k in range(2):
                    head_values(2 + k, i, k)
                    sub_newton(k, i)
                own.leave((HEADS - 2) // 2)
            sub_newton(HEADS - 2, None)
            sub_newton(HEADS - 1, None)
            accumulate(N_M1)
            accumulate(N_FINAL, NCH - 1)
            pool.wait_ge(rstd_done, N_FINAL + 2)
            for m in POOL_OUT:
                pool.wait_ge(gained, m + 1)
                nc.gpsimd.tensor_tensor(att[:, m, :], att[:, m, :], rstd[:, :],
                                        ALU.mult).then_inc(out_pool, 1)

        @block.scalar
        def _(act):
            own = Own(act, act_own)
            def split_hi(t, i=None, per=0):
                if i is None and t >= TILES:
                    return
                act.wait_ge(raw_in[t % RAWS], at(16 * (t // RAWS + 1), i, 16 * per // RAWS))
                if i is not None or t >= RING:
                    act.wait_ge(tile_done, at(t - RING + 1, i, per))
                nc.scalar.activation(w_hi[:, t % RING, :], w_raw[:, t % RAWS, :],
                                     ACT.Copy).then_inc(whi_done, 1)

            def operand_hi(dst, m, gain):
                nc.scalar.activation(dst[:, m, :], x[:, m, :], ACT.Copy,
                                     scale=gain).then_inc(ohi_done, 1)

            def square(n, m):
                k = n * NCH + m
                if k >= 2:
                    act.wait_ge(acc_done, k - 1)
                nc.scalar.activation(work[:, m % 2, :], x[:, m, :], ACT.Square).then_inc(sq_done, 1)

            def guess(g, psum, scale, eps, ln_done, exp_done):
                nc.scalar.activation(g, psum, ACT.Ln, scale=scale, bias=eps_col[:, eps:eps + 1]
                                     ).then_inc(ln_done[0], 1)
                act.wait_ge(*ln_done)
                nc.scalar.activation(g, g, ACT.Exp, scale=-0.5).then_inc(exp_done, 1)

            def norm_guess(n):
                act.wait_ge(stats_done, n + 1)
                k = n + (n > N_KV)
                guess(work[:, 3, :], ps[:, BANK_STATS, :], 1.0 / D, 0, (ln_done, k + 1), guess_done)
                if n == N_KV:
                    guess(cols[:, 1, :], ps[:, BANK_COLS, 0:QB], 1.0 / D, 0, (ln_done, k + 2),
                          guess_done)

            nc.scalar.preload_act_table_set("natural_log_exp_and_others")
            act.wait_ge(vec_in, 16)
            for m in range(NCH):
                act.wait_ge(x_in[m], 16)
                operand_hi(h_hi, m, col("a_norm", m))
                if m < 2:
                    split_hi(m)
                if m == 4:
                    nc.scalar.dma_start(gw_raw, gate_weights).then_inc(gw_in, 16)
                if m == NCH - 2:
                    split_hi(2)
                square(N_A, m)
            nc.scalar.dma_start(lam_in[:, :], lam_vecs).then_inc(lam_loaded, 16)
            act.wait_ge(decay_done, 1)
            nc.scalar.activation(small[:, 1, :], small[:, 0, :], ACT.Exp, scale=-1.0).then_inc(decay_done, 1)
            split_hi(3)
            act.wait_ge(consts_done, 1)
            norm_guess(N_A)
            act.wait_ge(gw_in, 16)
            nc.scalar.activation(gw_hi, gw_raw, ACT.Copy).then_inc(gwhi_done, 1)
            split_hi(RING)

            def xb_bias(m):
                act.wait_ge(bank_read, T_XB + m + 1)
                if m >= 2:
                    act.wait_ge(conv_done, m - 1)
                nc.scalar.activation(xb_pad[m % 2][:, PAD:], zr[m % 2], ACT.Identity,
                                     bias=col("b_in", m)).then_inc(xb_done, 1)

            def gate_sigmoids(m):
                act.wait_ge(gates_mm, m + 1)
                bank_r, bank_i = BANK_GATES[m % 2]
                nc.scalar.activation(lru_r[:, m, :], ps[:, bank_r, :], ACT.Sigmoid,
                                     bias=col("gate_b", m))
                nc.scalar.activation(lru_x[:, m, :], ps[:, bank_i, :], ACT.Sigmoid,
                                     bias=col("gate_b", NCH + m)).then_inc(gates_act, 1)

            xb_bias(0)
            for m in range(NCH):
                act.wait_ge(conv_done, m + 1)
                if m >= 2:
                    act.wait_ge(gates_mm, m - 1)
                nc.scalar.activation(xc_hi[m % 2], xc[m % XC], ACT.Copy).then_inc(xchi_done, 1)
                if m < NCH - 1:
                    xb_bias(m + 1)
                if m:
                    split_hi(T_XB + m + RING)
                    gate_sigmoids(m - 1)

            def gated_hi(c):
                act.wait_ge(hs_done, c + 1)
                nc.scalar.activation(u_hi[:, c, :], lru_v[:, c, :], ACT.Copy).then_inc(ohi_done, 1)

            def y_squared(m):
                act.wait_ge(bank_read, T_YB + m + 1)
                if m == 0:
                    act.wait_ge(gwlo_done, 1)
                nc.scalar.activation(gelu[:, m, :], work[:, m % 2, :], ACT.Identity,
                                     bias=col("b_in", NCH + m)).then_inc(y_done, 1)
                act.wait_ge(y_done, m + 1)
                if m >= 2:
                    act.wait_ge(gelu_done, m - 1)
                nc.scalar.activation(work[:, 2 + m % 2, :], gelu[:, m, :],
                                     ACT.Square).then_inc(ysq_done, 1)

            y_squared(0)
            for m in range(NCH):
                if m == 0:
                    gate_sigmoids(NCH - 1)
                    act.wait_ge(ix_done, NCH)
                    act.wait_ge(decay_done, 3)
                    act.wait_ge(gates_act, NCH)
                if m == 0:
                    split_hi(T_YB + RING)
                for c in DECAY_AT.get(m, ()):
                    own.step(nc.scalar.activation(lru_v[:, c, :], lru_r[:, c, :], ACT.Tanh,
                                                  scale=small[:, 8, c:c + 1]))
                    own.wait()
                    nc.scalar.activation(lru_r[:, c, :], lru_r[:, c, :], ACT.Exp,
                                         scale=small[:, 9, c:c + 1]).then_inc(lru_exp, 1)
                    if c == 3:
                        split_hi(T_YB + RING + 1)
                    if c == 5:
                        split_hi(T_YB + RING + 2)
                for c in GATED_AT.get(m - 1, ()):
                    gated_hi(c)
                act.wait_ge(arg_done, m + 1)
                nc.scalar.activation(work[:, 2 + m % 2, :], work[:, 2 + m % 2, :], ACT.Tanh,
                                     scale=GELU_C * GELU_CUBIC).then_inc(tanh_done, 1)
                if m < NCH - 1:
                    y_squared(m + 1)
                if m == SQRT_AT:
                    split_hi(T_OUT - 1)
                if m == SQRT_AT:
                    for c in range(NCH):
                        act.wait_ge(lru_q, c + 1)
                        nc.scalar.activation(lru_v[:, c, :], lru_v[:, c, :], ACT.Sqrt,
                                             scale=-1.0).then_inc(sqrt_done, 1)
                    split_hi(T_OUT)
                if m in SPLIT_AT:
                    split_hi(SPLIT_AT[m])
            gated_hi(NCH - 1)
            nc.scalar.preload_act_table_set("natural_log_exp_and_others")

            def residual_step(t, n, gains):
                for m in range(NCH):
                    act.wait_ge(bank_read, t + m + 1)
                    if gains is not None:
                        operand_hi(h_hi, m, col(gains[0], gains[1] + m))
                    square(n, m)
                    split_hi(t + m + RING)

            residual_step(T_OUT, N_M0, ("mlp_norm", 0))

            def mlp_up(t0, o0, i, norm=None):
                per = 2 * NCH
                for m in range(NCH):
                    if m == 0 and norm is not None:
                        split_hi(t0 + RING)
                        norm_guess(norm)
                    act.wait_ge(bank_read, at(t0 + m + 1, i, per))
                    nc.scalar.activation(work[:, 2 + m % 2, :], work[:, m % 2, :],
                                         ACT.Square).then_inc(sq_u_done, 1)
                    act.wait_ge(sq_u_done, at(o0 + m + 1, i, NCH))
                    nc.scalar.activation(u_hi[:, m, :], work[:, 2 + m % 2, :],
                                         ACT.Copy).then_inc(ohi_done, 1)
                    if m or norm is None:
                        split_hi(t0 + m + RING, i, per)

            def mlp(layer, t0, n_stats, n, gains):
                first_u = layer * NCH * GROUPS
                mlp_up(t0, first_u, None, n_stats)
                with act.Fori(0, GROUPS - 1) as i:
                    for m in range(NCH):
                        split_hi(t0 + NCH + m + RING, i, 2 * NCH)
                    mlp_up(t0 + 2 * NCH, first_u + NCH, i)
                residual_step(t0 + (2 * GROUPS - 1) * NCH, n, gains)

            mlp(0, T_MLP0, N_M0, N_KV, ("kv_norm", 0))

            act.wait_ge(lam_prod, 2)
            nc.scalar.activation(lam_s[:, 2:4], lam_s[:, 0:2], ACT.Exp).then_inc(lam_exp, 1)
            for m in range(NCH):
                operand_hi(u_hi, m, col("b_norm", m))
                split_hi(T_V + m + RING)
                if m == 0:
                    norm_guess(N_KV)
            for t in (T_KQ, T_KQ + 1):
                split_hi(t + RING)

            def exps(h, i, j):
                a = QB * h + j
                n = (QB - j) * P
                act.wait_ge(scores_read, at(2 * a + 2, i, 4 * QB))
                for c in range(2):
                    ins = nc.scalar.activation(prob[:, j % 2, c, 0:n], prob[:, j % 2, c, 0:n], ACT.Exp,
                                               scale=-1.0, bias=neg_min[:, j % 2, c:c + 1],
                                               accum_out=total[:, j % 2, c:c + 1])
                ins.then_inc(exp_done, 1)

            def transposed(h, i, j):
                a = QB * h + j
                qb = QB - 1 - j
                act.wait_ge(trans_mm, at(a + 1, i, 2 * QB))
                if j == 0 and (i is not None or h > 0):
                    act.wait_ge(att_mm, at(h, i, 2))
                nc.scalar.activation(
                    prob_t[:, 0:qb + 1, qb * P:(qb + 1) * P],
                    ps[:, BANK_T, 0:(qb + 1) * P].rearrange("p (b q) -> p b q", q=P),
                    ACT.Copy).then_inc(trans_read, 1)

            def att_out(h, i):
                act.wait_ge(att_mm, at(h + 1, i, 2))
                if i is not None or h > 0:
                    act.wait_ge(att_done, at(h, i, 2))
                nc.scalar.activation(o_raw[:, :], ps[:, BANK_O, :], ACT.Copy)
                nc.scalar.activation(sub[:, 0, :], ps[:, BANK_O, :], ACT.Square).then_inc(att_read, 1)

            def sub_guess_of(h, i):
                act.wait_ge(sub_mm, at(h + 1, i, 2))
                own.step(nc.scalar.activation(sub[:, 0, :], ps[:, BANK_O, :], ACT.Copy,
                                              scale=0.5 / V_DIM, bias=0.5 * SUBLN_EPS))
                own.wait()
                nc.scalar.activation(sub[:, 1, :], sub[:, 0, :], ACT.Ln, scale=2.0
                                     ).then_inc(sub_read, 1)
                act.wait_ge(sub_read, at(h + 1, i, 2))
                own.step(nc.scalar.activation(sub[:, 1, :], sub[:, 1, :], ACT.Exp, scale=-0.5))
                own.wait()
                nc.scalar.activation(sub[:, 2, :], sub[:, 1, :], ACT.Square).then_inc(sub_guess, 1)

            def attended_hi(m):
                act.wait_ge(att_done, m + 1)
                nc.scalar.activation(u_hi[:, m, :], att[:, m, :], ACT.Copy).then_inc(ohi_done, 1)

            def head(h, i, first=False, last=False):
                t = T_KQ + 2 * h + 2
                if not first:
                    att_out(h - 1, i)
                exps(h, i, 0)
                exps(h, i, 1)
                if last:
                    for m in range(HEADS - 2):
                        attended_hi(m)
                if not first:
                    sub_guess_of(h - 1, i)
                exps(h, i, 2)
                transposed(h, i, 0)
                if not last:
                    split_hi(t + RING, i, 4)
                exps(h, i, 3)
                for j in range(1, QB):
                    transposed(h, i, j)
                if not last:
                    split_hi(t + 1 + RING, i, 4)

            head(0, None, first=True)
            with act.Fori(0, (HEADS - 2) // 2) as i:
                own.enter(i, 4)
                head(1, i)
                head(2, i)
                own.leave((HEADS - 2) // 2)
            head(HEADS - 1, None, last=True)
            att_out(HEADS - 1, None)
            sub_guess_of(HEADS - 1, None)
            attended_hi(HEADS - 2)
            attended_hi(HEADS - 1)
            residual_step(T_O, N_M1, ("mlp_norm", NCH))
            mlp(1, T_MLP1, N_M1, N_FINAL, None)
            for m in range(NCH - 1):
                nc.scalar.activation(att[:, m, :], x[:, m, :], ACT.Copy,
                                     scale=col("final_norm", m)).then_inc(gained, 1)
            norm_guess(N_FINAL)
            m = NCH - 1
            nc.scalar.activation(att[:, m, :], x[:, m, :], ACT.Copy,
                                 scale=col("final_norm", m)).then_inc(gained, 1)

        @block.vector
        def _(dve):
            own = Own(dve, dve_own)

            def split_lo(t, i=None, per=0):
                if i is None and t >= TILES:
                    return
                dve.wait_ge(whi_done, at(t + 1, i, per))
                nc.vector.tensor_tensor(w_lo[:, t % RING, :], w_raw[:, t % RAWS, :],
                                        w_hi[:, t % RING, :], ALU.subtract).then_inc(wlo_done, 1)

            def operand_lo(dst_lo, dst_hi, m, gain, o):
                dve.wait_ge(ohi_done, o + 1)
                nc.vector.scalar_tensor_tensor(out=dst_lo[:, m, :], in0=x[:, m, :], scalar=gain,
                                               in1=dst_hi[:, m, :], op0=ALU.mult,
                                               op1=ALU.subtract).then_inc(olo_done, 1)

            dve.wait_ge(vec_in, 16)
            lam = vec[:, COLS["lambda"]:COLS["lambda"] + NCH]
            own.step(nc.vector.tensor_scalar(small[:, 7, :], lam, -1.0, None, ALU.mult))
            own.wait()
            nc.vector.tensor_tensor(small[:, 0, :], lam, small[:, 7, :], ALU.max).then_inc(decay_done, 1)
            for m in range(NCH):
                dve.wait_ge(x_in[m], 16)
                operand_lo(h_lo, h_hi, m, col("a_norm", m), O_A + m)
                if m < 2:
                    split_lo(m)
                if m == NCH - 2:
                    split_lo(2)
            split_lo(3)

            def newton(psum, v, g, tmp, result, k):
                dve.wait_ge(ln_done, k + 1)
                own.step(nc.vector.tensor_scalar(v, psum, -0.5 / D, -0.5 * NORM_EPS, ALU.mult, ALU.add))
                dve.wait_ge(guess_done, k + 1)
                own.wait()
                own.step(nc.vector.tensor_tensor(tmp, g, v, ALU.mult))
                own.wait()
                own.step(nc.vector.tensor_tensor(tmp, tmp, g, ALU.mult))
                own.wait()
                nc.vector.scalar_tensor_tensor(out=result, in0=tmp, scalar=1.5, in1=g, op0=ALU.add,
                                               op1=ALU.mult).then_inc(rstd_done, 1)
                dve.wait_ge(rstd_done, k + 1)

            def norm_newton(n):
                k = n + (n > N_KV)
                newton(ps[:, BANK_STATS, :], work[:, 2, :], work[:, 3, :], work[:, 1, :], rstd[:, :], k)
                if n == N_KV:
                    newton(ps[:, BANK_COLS, 0:QB], cols[:, 0, :], cols[:, 1, :], cols[:, 2, :],
                           rstd_col[:, :], k + 1)


            def decay():
                dve.wait_ge(decay_done, 2)
                own.step(nc.vector.tensor_scalar(small[:, 2, :], small[:, 1, :], 2.0, None, ALU.add))
                own.wait()
                own.step(nc.vector.reciprocal(small[:, 3, :], small[:, 2, :]))
                own.wait()
                own.step(nc.vector.tensor_tensor(small[:, 4, :], small[:, 1, :], small[:, 3, :], ALU.mult))
                own.wait()
                own.step(nc.vector.tensor_tensor(small[:, 5, :], small[:, 4, :], small[:, 4, :], ALU.mult))
                own.wait()
                own.step(nc.vector.tensor_scalar(small[:, 6, :], small[:, 5, :], 1.0 / 17.0, None, ALU.mult))
                own.wait()
                for k in range(15, 1, -2):
                    own.step(nc.vector.scalar_tensor_tensor(
                        out=small[:, 6, :], in0=small[:, 6, :], scalar=1.0 / k, in1=small[:, 5, :],
                        op0=ALU.add, op1=ALU.mult))
                    own.wait()
                own.step(nc.vector.scalar_tensor_tensor(
                    out=small[:, 6, :], in0=small[:, 6, :], scalar=1.0, in1=small[:, 4, :],
                    op0=ALU.add, op1=ALU.mult))
                own.step(nc.vector.tensor_scalar(small[:, 7, :], small[:, 7, :], 0.0, None, ALU.max))
                own.wait()
                own.step(nc.vector.scalar_tensor_tensor(
                    out=small[:, 7, :], in0=small[:, 6, :], scalar=2.0, in1=small[:, 7, :],
                    op0=ALU.mult, op1=ALU.add))
                own.wait()
                own.step(nc.vector.tensor_scalar(small[:, 8, :], small[:, 7, :], LRU_C / 2, None, ALU.mult))
                nc.vector.tensor_scalar(small[:, 9, :], small[:, 7, :], -LRU_C, None,
                                        ALU.mult).then_inc(decay_done, 1)

            def branch(m):
                t = T_XB + m
                dve.wait_ge(tile_done, t + 1)
                if m >= 2:
                    dve.wait_ge(xb_done, m - 1)
                nc.vector.tensor_tensor(zr[m % 2], ps[:, t % RING, :], rstd[:, :],
                                        ALU.mult).then_inc(bank_read, 1)

            norm_newton(N_A)
            branch(0)
            for m in range(NCH):
                dve.wait_ge(xb_done, m + 1)
                if m >= XC:
                    dve.wait_ge(ix_done, m - XC + 1)
                pad = xb_pad[m % 2]
                own.step(nc.vector.tensor_scalar(xc[m % XC], pad[:, PAD:PAD + S],
                                                 col("conv_w", PAD * NCH + m), col("conv_b", m),
                                                 ALU.mult, ALU.add))
                for j in range(PAD - 1, -1, -1):
                    own.wait()
                    ins = nc.vector.scalar_tensor_tensor(
                        out=xc[m % XC], in0=pad[:, j:j + S], scalar=col("conv_w", j * NCH + m),
                        in1=xc[m % XC], op0=ALU.mult, op1=ALU.add)
                    if j:
                        own.step(ins)
                    else:
                        ins.then_inc(conv_done, 1)
                if m < NCH - 1:
                    branch(m + 1)
                dve.wait_ge(xchi_done, m + 1)
                nc.vector.tensor_tensor(xc_lo[m % 2], xc[m % XC], xc_hi[m % 2],
                                        ALU.subtract).then_inc(xclo_done, 1)
                if m == 3:
                    decay()

            def gelu_gate(m):
                dve.wait_ge(tanh_done, m + 1)
                nc.vector.scalar_tensor_tensor(
                    out=gelu[:, m, :], in0=work[:, 2 + m % 2, :], scalar=1.0, in1=gelu[:, m, :],
                    op0=ALU.add, op1=ALU.mult).then_inc(gelu_done, 1)

            def recurrence(c):
                dve.wait_ge(bx_done, c + 1)
                dve.wait_ge(lru_a, c + 1)
                own.step(nc.vector.tensor_tensor_scan(
                    lru_v[:, c, :], lru_r[:, c, :], lru_x[:, c, :], 0.0, ALU.mult, ALU.add))

            def gated(c):
                own.wait()
                dve.wait_ge(gelu_done, c + 1)
                nc.vector.scalar_tensor_tensor(out=lru_v[:, c, :], in0=lru_v[:, c, :], scalar=0.5,
                                               in1=gelu[:, c, :], op0=ALU.mult,
                                               op1=ALU.mult).then_inc(hs_done, 1)

            def y_scaled(m):
                t = T_YB + m
                dve.wait_ge(tile_done, t + 1)
                if m >= 2:
                    dve.wait_ge(y_done, m - 1)
                nc.vector.tensor_tensor(work[:, m % 2, :], ps[:, t % RING, :], rstd[:, :],
                                        ALU.mult).then_inc(bank_read, 1)

            y_scaled(0)
            for m in range(NCH):
                dve.wait_ge(ysq_done, m + 1)
                nc.vector.scalar_tensor_tensor(
                    out=work[:, 2 + m % 2, :], in0=work[:, 2 + m % 2, :], scalar=1.0 / GELU_CUBIC,
                    in1=gelu[:, m, :], op0=ALU.add, op1=ALU.mult).then_inc(arg_done, 1)
                if m < NCH - 1:
                    y_scaled(m + 1)
                for c in DECAY_AT.get(m, ()):
                    dve.wait_ge(lru_exp, c + 1)
                    own.step(nc.vector.scalar_tensor_tensor(
                        out=lru_r[:, c, :], in0=lru_r[:, c, :], scalar=1.0, in1=lru_v[:, c, :],
                        op0=ALU.add, op1=ALU.mult))
                    own.wait()
                    nc.vector.scalar_tensor_tensor(
                        out=lru_v[:, c, :], in0=lru_r[:, c, :], scalar=-2.0, in1=lru_r[:, c, :],
                        op0=ALU.add, op1=ALU.mult).then_inc(lru_q, 1)
                for c in SCAN_AT.get(m, ()):
                    recurrence(c)
                if m == SQRT_AT + 1:
                    dve.wait_ge(wlo_done, T_OUT)
                    split_lo(T_OUT)
                gelu_gate(m)
                for c in GATED_AT.get(m, ()):
                    gated(c)
                if m in SPLIT_AT and SPLIT_AT[m] < T_OUT + RING - 1:
                    split_lo(SPLIT_AT[m])
            dve.wait_ge(olo_done, O_Y + NCH - 1)
            dve.wait_ge(ohi_done, O_Y + NCH)
            nc.vector.tensor_tensor(u_lo[:, NCH - 1, :], lru_v[:, NCH - 1, :], u_hi[:, NCH - 1, :],
                                    ALU.subtract).then_inc(olo_done, 1)

            def residual_step(t, o0, gains):
                for m in range(NCH):
                    dve.wait_ge(tile_done, t + m + 1)
                    nc.vector.tensor_tensor(x[:, m, :], x[:, m, :], ps[:, (t + m) % RING, :],
                                            ALU.add).then_inc(bank_read, 1)
                    split_lo(t + m + RING - 1)
                    if gains is not None:
                        operand_lo(h_lo, h_hi, m, col(gains[0], gains[1] + m), o0 + m)

            residual_step(T_OUT, O_M0, ("mlp_norm", 0))

            def mlp_up(t0, u0, o0, i, norm=None):
                per = 2 * NCH
                for m in range(NCH):
                    t = t0 + m
                    if m == 0 and norm is not None:
                        split_lo(t + RING - 1)
                        norm_newton(norm)
                    dve.wait_ge(tile_done, at(t + 1, i, per))
                    if u0 + m >= 2:
                        dve.wait_ge(sq_u_done, at(u0 + m - 1, i, NCH))
                    nc.vector.scalar_tensor_tensor(
                        out=work[:, m % 2, :], in0=ps[:, t % RING, :], scalar=0.0, in1=rstd[:, :],
                        op0=ALU.max, op1=ALU.mult).then_inc(bank_read, 1)
                    if m or norm is None:
                        split_lo(t + RING - 1, i, per)
                    dve.wait_ge(ohi_done, at(o0 + m + 1, i, NCH))
                    nc.vector.tensor_tensor(u_lo[:, m, :], work[:, 2 + m % 2, :], u_hi[:, m, :],
                                            ALU.subtract).then_inc(olo_done, 1)

            def mlp(layer, t0, n_stats, o_next, gains):
                u0 = layer * NCH * GROUPS
                o0 = O_U1 if layer else O_U0
                mlp_up(t0, u0, o0, None, n_stats)
                with dve.Fori(0, GROUPS - 1) as i:
                    for m in range(NCH):
                        t = t0 + NCH + m
                        dve.wait_ge(tile_done, at(t + 1, i, 2 * NCH))
                        nc.vector.tensor_tensor(x[:, m, :], x[:, m, :], ps[:, t % RING, :],
                                                ALU.add).then_inc(bank_read, 1)
                        split_lo(t + RING - 1, i, 2 * NCH)
                    mlp_up(t0 + 2 * NCH, u0 + NCH, o0 + NCH, i)
                residual_step(t0 + (2 * GROUPS - 1) * NCH, o_next, gains)

            mlp(0, T_MLP0, N_M0, O_KV, ("kv_norm", 0))

            dve.wait_ge(lam_loaded, 16)
            for k in range(2):
                nc.vector.tensor_tensor_reduce(
                    out=lam_tmp[:, :], in0=lam_in[:, 2 * k * HEAD_DIM:(2 * k + 1) * HEAD_DIM],
                    in1=lam_in[:, (2 * k + 1) * HEAD_DIM:(2 * k + 2) * HEAD_DIM], scale=1.0, scalar=0.0,
                    op0=ALU.mult, op1=ALU.add, accum_out=lam_s[:, k:k + 1]).then_inc(lam_prod, 1)
                dve.wait_ge(lam_prod, k + 1)
            dve.wait_ge(lam_exp, 1)
            own.step(nc.vector.tensor_tensor(lam_s[:, 4:5], lam_s[:, 3:4], lam_s[:, 2:3], ALU.subtract))
            own.wait()
            own.step(nc.vector.tensor_scalar(lam_s[:, 5:6], lam_s[:, 4:5], LAM_INIT, None, ALU.subtract))
            own.step(nc.vector.tensor_scalar(lam_s[:, 6:7], col("subln"), 1.0 - LAM_INIT, None, ALU.mult))
            own.wait()
            neg_lam, sub_gain = lam_s[:, 5:6], lam_s[:, 6:7]

            for half in range(2):
                for s in range(4):
                    m = half * 4 + s
                    split_lo(T_V + m + RING - 1)
                    operand_lo(u_lo, u_hi, m, col("b_norm", m), O_Q + m)
                    if m == 0:
                        norm_newton(N_KV)
                dve.wait_ge(tile_done, T_V + 4 * half + 4)
                for tok in range(QB):
                    nc.vector.tensor_scalar(value[:, tok, half * S:(half + 1) * S],
                                            ps[:, 4 * half + tok, :], rstd_col[:, tok:tok + 1], None,
                                            ALU.mult).then_inc(bank_read, 1)

            def key(h, i):
                t = T_KQ + 2 * h
                dve.wait_ge(tile_done, at(t + 1, i, 4))
                nc.vector.tensor_tensor(kq[:, h % 2, 0, :], ps[:, 0, :], rstd[:, :],
                                        ALU.mult).then_inc(bank_read, 1)
                split_lo(t + RING - 1, i, 4)

            def query(h, i):
                t = T_KQ + 2 * h + 1
                dve.wait_ge(tile_done, at(t + 1, i, 4))
                nc.vector.scalar_tensor_tensor(out=kq[:, h % 2, 1, :], in0=ps[:, 1, :],
                                               scalar=-HEAD_DIM ** -0.5, in1=rstd[:, :], op0=ALU.mult,
                                               op1=ALU.mult).then_inc(bank_read, 1)
                split_lo(t + RING - 1, i, 4)

            def biased(h, i, j):
                a = QB * h + j
                n = (QB - j) * P
                dve.wait_ge(scores_mm, at(a + 1, i, 2 * QB))
                if i is not None or a >= 2:
                    dve.wait_ge(trans_mm, at(a - 1, i, 2 * QB))
                nc.vector.memset(absorb[:, j % 2:j % 2 + 1], 0.0)
                for c in range(2):
                    nc.vector.tensor_tensor_reduce(
                        out=prob[:, j % 2, c, 0:n], in0=ps[:, BANK_SCORES + 2 * (j % 2) + c, 0:n],
                        in1=bias[:, S - n:S], scale=1.0, scalar=MASKED, op0=ALU.add, op1=ALU.min,
                        accum_out=neg_min[:, j % 2, c:c + 1]).then_inc(scores_read, 1)

            def combined(h, i, j):
                a = QB * h + j
                n = (QB - j) * P
                s = j % 2
                dve.wait_ge(exp_done, at(a + 1, i, 2 * QB))
                own.step(nc.vector.reciprocal(inv[:, s, :], total[:, s, :]))
                own.wait()
                own.step(nc.vector.tensor_tensor(inv_lam[:, s:s + 1], inv[:, s, 1:2], neg_lam, ALU.mult))
                own.wait()
                own.step(nc.vector.tensor_scalar(prob[:, s, 1, 0:n], prob[:, s, 1, 0:n],
                                                 inv_lam[:, s:s + 1], None, ALU.mult))
                own.wait()
                nc.vector.scalar_tensor_tensor(out=prob[:, s, 0, 0:n], in0=prob[:, s, 0, 0:n],
                                               scalar=inv[:, s, 0:1], in1=prob[:, s, 1, 0:n],
                                               op0=ALU.mult, op1=ALU.add).then_inc(prob_done, 1)

            def normed(h, i):
                dve.wait_ge(sub_rstd, at(h + 1, i, 2))
                dst = att[:, h, :] if i is None else \
                    att[:, bass.ds(i * 2 + h, 1), :].rearrange("p o s -> p (o s)")
                nc.vector.scalar_tensor_tensor(out=dst, in0=o_raw[:, :], scalar=sub_gain,
                                               in1=sub[:, 2, :], op0=ALU.mult,
                                               op1=ALU.mult).then_inc(att_done, 1)

            OWN_PER_HEAD = 3 * QB + 1

            def attended_lo(m):
                dve.wait_ge(ohi_done, O_ATT + m + 1)
                nc.vector.tensor_tensor(u_lo[:, m, :], att[:, m, :], u_hi[:, m, :],
                                        ALU.subtract).then_inc(olo_done, 1)

            def head(h, i, first=False, last=False):
                biased(h, i, 0)
                biased(h, i, 1)
                combined(h, i, 0)
                if last:
                    for m in range(HEADS - 2):
                        attended_lo(m)
                biased(h, i, 2)
                combined(h, i, 1)
                if not last:
                    key(h + 1, i)
                biased(h, i, 3)
                dve.wait_ge(scores_read, at(2 * QB * (h + 1), i, 4 * QB))
                own.step(nc.vector.tensor_scalar(bias[:, :], bias[:, :], 0.5, None, ALU.mult))
                combined(h, i, 2)
                combined(h, i, 3)
                if not last:
                    query(h + 1, i)
                if not first:
                    normed(h - 1, i)

            key(0, None)
            query(0, None)
            dve.wait_ge(consts_done, 3)
            head(0, None, first=True)
            with dve.Fori(0, (HEADS - 2) // 2) as i:
                own.enter(i, 2 * OWN_PER_HEAD)
                head(1, i)
                head(2, i)
                own.leave((HEADS - 2) // 2)
            head(HEADS - 1, None, last=True)
            attended_lo(HEADS - 2)
            normed(HEADS - 1, None)
            attended_lo(HEADS - 1)
            residual_step(T_O, O_M1, ("mlp_norm", NCH))
            mlp(1, T_MLP1, N_M1, None, None)
            norm_newton(N_FINAL)
            for n, m in enumerate(DVE_OUT):
                dve.wait_ge(gained, m + 1)
                ins = nc.vector.tensor_tensor(att[:, m, :], att[:, m, :], rstd[:, :], ALU.mult)
                ins.then_inc(out_dve, 1)

        @block.tensor
        def _(pe):
            def passes(bank, slot, hi, lo, k, parts=(0, 1, 2)):
                ws = slice(k * P, (k + 1) * P)
                pairs = ((w_hi, hi), (w_hi, lo), (w_lo, hi))
                for n in parts:
                    w, o = pairs[n]
                    ins = nc.tensor.matmul(ps[:, bank, :], w[:, slot, ws], o[:, k, :],
                                           start=(k == 0 and n == 0), stop=(k == NCH - 1 and n == 2))
                return ins

            def tile_starts(t, free, i=None, per=0):
                pe.wait_ge(wlo_done, at(t + 1, i, per))
                if i is not None or free > 0:
                    pe.wait_ge(bank_read, at(free, i, per))

            def tile(t, hi, lo, o=None, i=None, per=0, o_per=0):
                tile_starts(t, t - RING + 1, i, per)
                for k in range(NCH):
                    if o is not None:
                        pe.wait_ge(olo_done, at(o + k + 1, i, o_per))
                    ins = passes(t % RING, t % RING, hi, lo, k)
                ins.then_inc(tile_done, 1)

            def open_tiles(t0, n, hi, lo, o):
                for k in range(NCH):
                    for t in range(t0, t0 + n):
                        if k == 0:
                            tile_starts(t, t - RING + 1)
                        pe.wait_ge(olo_done, o + k + 1)
                        ins = passes(t % RING, t % RING, hi, lo, k)
                        if k == NCH - 1:
                            ins.then_inc(tile_done, 1)

            def stats(n):
                final = n == N_FINAL
                pe.wait_ge(acc_done, (n + 1) * NCH - final)
                ins = nc.tensor.matmul(ps[:, BANK_STATS, :], ones[:, :], acc[:, :], start=True,
                                       stop=not final)
                if final:
                    pe.wait_ge(sq_done, (n + 1) * NCH)
                    ins = nc.tensor.matmul(ps[:, BANK_STATS, :], ones[:, :], work[:, 1, :],
                                           start=False, stop=True)
                if n == N_KV:
                    for tok in range(QB):
                        ins = nc.tensor.matmul(ps[:, BANK_COLS, tok:tok + 1],
                                               acc[:, tok * P:(tok + 1) * P], ones[:, 0:1],
                                               start=True, stop=True)
                ins.then_inc(stats_done, 1)

            def gates(m):
                pe.wait_ge(xclo_done, m + 1)
                if m == 0:
                    pe.wait_ge(gwlo_done, 1)
                if m == 1:
                    pe.wait_ge(rstd_done, N_A + 1)
                if m >= 2:
                    pe.wait_ge(gates_act, m - 1)
                for g, bank in enumerate(BANK_GATES[m % 2]):
                    ws = slice((g * NCH + m) * P, (g * NCH + m + 1) * P)
                    for n, (w, o) in enumerate(((gw_hi, xc_hi), (gw_hi, xc_lo), (gw_lo, xc_hi))):
                        ins = nc.tensor.matmul(ps[:, bank, :], w[:, ws], o[m % 2],
                                               start=(n == 0), stop=(n == 2))
                ins.then_inc(gates_mm, 1)

            pe.wait_ge(consts_done, 1)
            for _ in range(WARM_UP):
                nc.tensor.matmul(ps[:, BANK_STATS, :], ones[:, :], three_halves[:, :], start=True,
                                 stop=True)
            open_tiles(T_XB, 2, h_hi, h_lo, O_A)
            stats(N_A)
            gates_after = {3: (0,), 4: (1,), 5: (2, 3), 6: (4,), 7: (5,), 8: (6, 7)}
            for t in range(T_XB + 2, T_OUT):
                tile(t, h_hi, h_lo)
                for m in gates_after.get(t, ()):
                    gates(m)
            open_tiles(T_OUT, OPEN, u_hi, u_lo, O_Y)
            for m in range(OPEN, NCH):
                tile(T_OUT + m, u_hi, u_lo)

            def mlp(t0, o_h, o_u, n):
                per = 2 * NCH
                for m in range(NCH):
                    tile(t0 + m, h_hi, h_lo, o_h if m == 0 else None)
                    if m == 0:
                        stats(n)

                def down(first_t, first_o, i):
                    for m in range(NCH):
                        tile(first_t + m, u_hi, u_lo, first_o if m == 0 else None, i, per, NCH)

                with pe.Fori(0, GROUPS - 1) as i:
                    down(t0 + NCH, o_u, i)
                    for m in range(NCH):
                        tile(t0 + per + m, h_hi, h_lo, None, i, per)
                down(t0 + per * GROUPS - NCH, o_u + (GROUPS - 1) * NCH, None)

            mlp(T_MLP0, O_M0, O_U0, N_M0)

            for half in range(2):
                for s in range(4):
                    t = T_V + half * 4 + s
                    tile_starts(t, T_V)
                    if half == 1 and s == 0:
                        pe.wait_ge(rstd_done, N_KV + 2)
                    for kk in range(2):
                        k = 2 * s + kk
                        if half == 0:
                            pe.wait_ge(olo_done, O_KV + k + 1)
                        cs = slice(kk * S, (kk + 1) * S)
                        for tok in range(QB):
                            ts = slice(tok * P, (tok + 1) * P)
                            for n, (o, w) in enumerate(((h_hi, w_hi), (h_lo, w_hi), (h_hi, w_lo))):
                                ins = nc.tensor.matmul(ps[:, 4 * half + tok, :], o[:, k, ts], w[:, t % RING, cs],
                                                       start=(k == 0 and n == 0),
                                                       stop=(k == NCH - 1 and n == 2))
                    ins.then_inc(tile_done, 1)
                    if half == 0 and s == 0:
                        stats(N_KV)

            def kq_part(h, i, part):
                which, quarter = divmod(part, 4)
                t = T_KQ + 2 * h + which
                if quarter == 0:
                    tile_starts(t, t - 1 if h else T_V + 4, i, 4)
                for k in (2 * quarter, 2 * quarter + 1):
                    if which == 0:
                        ins = passes(0, t % RING, h_hi, h_lo, k)
                    else:
                        ins = passes(1, t % RING, u_hi, u_lo, k)
                if quarter == 3:
                    ins.then_inc(tile_done, 1)

            def scores(h, i, j):
                a = QB * h + j
                qb = QB - 1 - j
                n = (qb + 1) * P
                if j == 0:
                    pe.wait_ge(bank_read, at(T_KQ + 2 * h + 2, i, 4))
                if i is not None or a >= 2:
                    pe.wait_ge(scores_read, at(2 * (a - 1), i, 4 * QB))
                for c in range(2):
                    rows = slice(c * HEAD_DIM, (c + 1) * HEAD_DIM)
                    ins = nc.tensor.matmul(ps[:, BANK_SCORES + 2 * (j % 2) + c, 0:n],
                                           kq[rows, h % 2, 1, qb * P:(qb + 1) * P],
                                           kq[rows, h % 2, 0, 0:n], start=True, stop=True)
                ins.then_inc(scores_mm, 1)

            def transposes(h, i, j):
                a = QB * h + j
                qb = QB - 1 - j
                pe.wait_ge(prob_done, at(a + 1, i, 2 * QB))
                if i is not None or a >= 1:
                    pe.wait_ge(trans_read, at(a, i, 2 * QB))
                for kb in range(qb + 1):
                    ks = slice(kb * P, (kb + 1) * P)
                    ins = nc.tensor.transpose(ps[:, BANK_T, ks], prob[:, j % 2, 0, ks], ident[:, :])
                ins.then_inc(trans_mm, 1)

            def attend(h, i):
                pe.wait_ge(trans_read, at(QB * (h + 1), i, 2 * QB))
                pe.wait_ge(value_done, at(h + 1, i, 2))
                if i is not None or h > 0:
                    pe.wait_ge(sub_read, at(h, i, 2))
                for kb in range(QB):
                    ins = nc.tensor.matmul(ps[:, BANK_O, kb * P:S], value_h[:, h % 2, kb, :],
                                           prob_t[:, kb, kb * P:S], start=(kb == 0),
                                           stop=(kb == QB - 1), skip_group_check=True)
                ins.then_inc(att_mm, 1)

            def sub_sum(h, i):
                pe.wait_ge(att_read, at(h + 1, i, 2))
                nc.tensor.matmul(ps[:, BANK_O, :], ones[:, :], sub[:, 0, :], start=True,
                                 stop=True).then_inc(sub_mm, 1)

            def head(h, i, first=False, last=False):
                def part(n):
                    if not last:
                        kq_part(h + 1, i, n)
                    elif n % 4 < 3:
                        t = T_O + n // 4
                        if n % 4 == 0:
                            tile_starts(t, T_O)
                        for k in (2 * (n % 4), 2 * (n % 4) + 1):
                            pe.wait_ge(olo_done, O_ATT + k + 1)
                            passes(t % RING, t % RING, u_hi, u_lo, k)

                scores(h, i, 0)
                scores(h, i, 1)
                part(0)
                part(1)
                if not first:
                    sub_sum(h - 1, i)
                scores(h, i, 2)
                part(2)
                transposes(h, i, 0)
                part(3)
                scores(h, i, 3)
                part(4)
                transposes(h, i, 1)
                part(5)
                transposes(h, i, 2)
                part(6)
                transposes(h, i, 3)
                part(7)
                attend(h, i)

            for part in range(4):
                kq_part(0, None, part)
            pe.wait_ge(olo_done, O_Q + NCH)
            for part in range(4, 8):
                kq_part(0, None, part)
            pe.wait_ge(bank_read, T_KQ)
            pe.wait_ge(consts_done, 3)
            head(0, None, first=True)
            with pe.Fori(0, (HEADS - 2) // 2) as i:
                head(1, i)
                head(2, i)
            head(HEADS - 1, None, last=True)
            sub_sum(HEADS - 1, None)

            pe.wait_ge(olo_done, O_ATT + HEADS - 1)
            for t in (T_O, T_O + 1):
                passes(t % RING, t % RING, u_hi, u_lo, HEADS - 2)
            for t in range(T_O + 2, T_O + OPEN):
                tile_starts(t, T_O)
                for k in range(HEADS - 1):
                    passes(t % RING, t % RING, u_hi, u_lo, k)
            pe.wait_ge(olo_done, O_ATT + HEADS)
            for t in range(T_O, T_O + OPEN):
                passes(t % RING, t % RING, u_hi, u_lo, HEADS - 1).then_inc(tile_done, 1)
            for m in range(OPEN, NCH):
                tile(T_O + m, u_hi, u_lo)
            mlp(T_MLP1, O_M1, O_U1, N_M1)
            stats(N_FINAL)


def kernel(**inputs):
    import concourse.bacc as bacc
    from concourse.bass_utils import run_bass_kernel_spmd

    a = {k: np.asarray(v) for k, v in inputs.items()}

    def by_output(w):
        n = w.shape[1] // P
        return w.reshape(NCH, P, n, P).transpose(2, 1, 0, 3).reshape(n, P, TILE)

    def by_input(w):
        return w.reshape(4, 2, P, S).transpose(0, 2, 1, 3).reshape(4, P, TILE)

    def mlp(layer):
        for g in range(GROUPS):
            yield by_output(a["mlp_w1"][layer][:, g * D:(g + 1) * D])
            yield by_output(a["mlp_w2"][layer][g * D:(g + 1) * D])

    keys, queries = by_output(a["w_kv"][:, :D]), by_output(a["b_w_q"][0])
    parts = [by_output(a["a_w_in"][0]), by_output(a["a_w_out"][0]), *mlp(0)]
    parts += [by_input(a["w_kv"][:, D + h * S:D + (h + 1) * S]) for h in range(2)]
    parts += [np.stack([keys, queries], axis=1).reshape(2 * HEADS, P, TILE)]
    parts += [by_output(a["b_w_o"][0]), *mlp(1)]
    weights = np.ascontiguousarray(np.concatenate(parts))

    def columns(v):
        return np.asarray(v).reshape(-1, P).T

    vectors = np.ascontiguousarray(np.concatenate([columns(a[n]) for n in (
        "a_norm", "a_b_in", "a_conv_w", "a_conv_b", "a_gate_b", "a_lambda", "kv_norm", "b_norm",
        "mlp_norm", "final_norm", "b_subln")], axis=1))
    arrays = {
        "x_t": np.ascontiguousarray(a["x"][0].T).reshape(NCH, P, S),
        "weights": weights,
        "gate_weights": np.ascontiguousarray(
            a["a_gate_w"][0].transpose(2, 0, 1, 3).reshape(P, 2 * NCH * P)),
        "vectors": vectors,
        "lam_vecs": np.ascontiguousarray(np.broadcast_to(a["b_lam"].reshape(1, -1), (P, 4 * HEAD_DIM))),
    }
    nc = bacc.Bacc("TRN2", target_bir_lowering=False, num_devices=1)
    f32 = mybir.dt.float32
    args = [nc.dram_tensor(n, v.shape, f32, kind="ExternalInput").ap() for n, v in arrays.items()]
    out = nc.dram_tensor("y_t", [NCH, P, S], f32, kind="ExternalOutput").ap()
    build(nc, *args, out)
    r = run_bass_kernel_spmd(nc, [arrays], core_ids=[0])
    y = r.results[0]["y_t"].reshape(D, S).T
    return np.ascontiguousarray(y).reshape(1, S, D)
```

```python
import math
from contextlib import ExitStack

import numpy as np

import concourse.bass as bass
from concourse import mybir

P = 128
D = 1024
S = 512
NCH = D // P
HEADS = 8
HEAD_DIM = D // HEADS // 2
V_DIM = 2 * HEAD_DIM
D_FF = 4 * D
GROUPS = D_FF // D
CONV_W = 4
TILE = NCH * P
QB = S // P
NORM_EPS = 1e-6
SUBLN_EPS = 1e-5
LRU_C = 8.0
LAM_INIT = 0.8 - 0.6 * math.exp(-0.3)
GELU_C = math.sqrt(2.0 / math.pi)
GELU_CUBIC = 0.044715
SLOPE_0 = 2.0 ** (-8.0 / HEADS)
MASKED = 3.0e38

T_XB = 0
T_YB = T_XB + NCH
T_OUT = T_YB + NCH
T_MLP0 = T_OUT + NCH
T_V = T_MLP0 + 2 * NCH * GROUPS
T_QK = T_V + NCH
T_O = T_QK + 2 * HEADS
T_MLP1 = T_O + NCH
TILES = T_MLP1 + 2 * NCH * GROUPS

O_A = 0
O_Y = O_A + NCH
O_M0 = O_Y + NCH
O_U0 = O_M0 + NCH
O_KV = O_U0 + NCH * GROUPS
O_Q = O_KV + NCH
O_ATT = O_Q + NCH
O_M1 = O_ATT + NCH
O_U1 = O_M1 + NCH

N_A, N_M0, N_KV, N_M1, N_FINAL = range(5)

COLS = {}
_at = 0
for _name, _n in (("a_norm", NCH), ("b_in", 2 * NCH), ("conv_w", CONV_W * NCH), ("conv_b", NCH),
                  ("gate_b", 2 * NCH), ("lambda", NCH), ("kv_norm", NCH), ("b_norm", NCH),
                  ("mlp_norm", 2 * NCH), ("final_norm", NCH), ("subln", 1)):
    COLS[_name] = _at
    _at += _n
NCOLS = _at

BANK_COLS, BANK_STATS = 6, 7
BANK_GATES = ((4, 5), (6, 7))
BANK_SCORES, BANK_T, BANK_O = 2, 6, 7
RING = 4
XC = 4
WARM_UP = 4
RAWS = 2
OPEN = 3
OPEN_ATT = 4
LAST_HEAD = ((T_O, (0, 1)), (T_O, (2, 3)), (T_O, (4, 5)), (T_O + 1, (0, 1)), (T_O + 1, (2, 3)),
             (T_O + 1, (4, 5)), (T_O + 2, (0, 1, 2)), (T_O + 2, (3, 4, 5)))
POOL_LO = range(RING, T_OUT)
DECAY_AT = {0: range(0, 4), 1: range(4, 8)}
Y_AT = {0: (1,), 1: (2,), 2: (3, 4), 3: (5,), 4: (6,), 5: (7,)}
SQRT_AT = 1
SCAN_AT = {2: (0, 1), 3: (2, 3), 4: (4, 5), 5: (6, 7)}
GATED_AT = {2: (0, 1), 3: (2, 3), 4: (4,), 5: (5,), 6: (6,), 7: (7,)}
SPLIT_AT = {2: (T_OUT + 1, T_OUT + 2), 6: (T_OUT + 3,)}
POOL_OUT = (1, 3, 5)
DVE_OUT = (0, 2, 4, 6, 7)
HALVES = (slice(0, S // 2), slice(S // 2, S))
BANK_LAST = (4, 5)
BANK_FINAL = (BANK_STATS, BANK_COLS)


def at(first, i, per):
    return first if i is None else i * per + first


def build(nc, x_t, weights, gate_weights, vectors, lam_vecs, out_t):
    F32 = mybir.dt.float32
    F32R = mybir.dt.float32r
    ACT = mybir.ActivationFunctionType
    ALU = mybir.AluOpType

    keep = ExitStack()
    with keep:
        def sb(name, shape, dt, stack=keep):
            return stack.enter_context(nc.sbuf_tensor(name, shape, dt))

        def sem(name):
            return keep.enter_context(nc.semaphore(name))

        x = sb("x", [P, NCH, S], F32)
        w_raw = sb("w_raw", [P, RAWS, TILE], F32)
        w_hi = sb("w_hi", [P, RING, TILE], F32R)
        w_lo = sb("w_lo", [P, RING, TILE], F32R)
        h_hi = sb("h_hi", [P, NCH, S], F32R)
        h_lo = sb("h_lo", [P, NCH, S], F32R)
        u_hi = sb("u_hi", [P, NCH, S], F32R)
        u_lo = sb("u_lo", [P, NCH, S], F32R)
        work = sb("work", [P, 4, S], F32)
        acc = sb("acc", [P, S], F32)
        rstd = sb("rstd", [P, S], F32)
        vec = sb("vec", [P, NCOLS], F32)
        small = sb("small", [P, 10, NCH], F32)
        cols = sb("cols", [P, 3, QB], F32)
        eps_col = sb("eps_col", [P, 1], F32)
        rstd_col = sb("rstd_col", [P, QB], F32)
        ones = sb("ones", [P, P], F32)
        three_halves = sb("three_halves", [P, S], F32)
        absorb = sb("absorb", [P, 2], F32)

        lru = ExitStack()
        lru_r = sb("lru_r", [P, NCH, S], F32, lru)
        lru_v = sb("lru_v", [P, NCH, S], F32, lru)
        lru_x = sb("lru_x", [P, NCH, S], F32, lru)
        gelu = sb("gelu", [P, NCH, S], F32, lru)
        lru.close()
        flat_v = lru_v[:, :, :].rearrange("p c s -> p (c s)")
        zr = [flat_v[:, (1 + i) * S:(2 + i) * S] for i in range(2)]
        PAD = CONV_W - 1
        xb_pad = [flat_v[:, 3 * S + i * (S + PAD):3 * S + (i + 1) * (S + PAD)] for i in range(2)]
        GW = 2 * NCH * P
        gw_raw = gelu[:, :, :].rearrange("p c s -> p (c s)")[:, 0:GW]
        gw_hi = u_hi[:, :, :].rearrange("p c s -> p (c s)")[:, 0:GW]
        gw_lo = u_lo[:, :, :].rearrange("p c s -> p (c s)")[:, 0:GW]
        xc = [lru_v[:, 6, :], lru_v[:, 7, :], gelu[:, GW // S, :], gelu[:, GW // S + 1, :]]
        xc_hi = [u_hi[:, GW // S + i, :] for i in range(2)]
        xc_lo = [u_lo[:, GW // S + i, :] for i in range(2)]

        value = sb("value", [P, QB, D], F32)
        att = sb("att", [P, HEADS, S], F32)
        prob = sb("prob", [P, 2, 2, S], F32)
        prob_t = sb("prob_t", [P, QB, S], F32)
        kq = sb("kq", [P, 2, S], F32)
        kq_hi = sb("kq_hi", [P, 2, S], F32R)
        kq_lo = sb("kq_lo", [P, 2, S], F32R)
        value_h = sb("value_h", [P, 2, QB, P], F32)
        bias = sb("bias", [P, S], F32)
        sub = work[:, 0:3, :]
        o_raw = work[:, 3, :]
        ident = sb("ident", [P, P], F32)
        lam_in = sb("lam_in", [P, 4 * HEAD_DIM], F32)
        lam_tmp = sb("lam_tmp", [P, HEAD_DIM], F32)
        lam_s = sb("lam_s", [P, 8], F32)
        neg_min = sb("neg_min", [P, 2, 2], F32)
        total = sb("total", [P, 2, 2], F32)
        inv = sb("inv", [P, 2, 2], F32)
        inv_lam = sb("inv_lam", [P, 2], F32)

        ps = keep.enter_context(nc.psum_tensor("ps", [P, 8, S], F32))

        x_in = [sem(f"x_in{i}") for i in range(NCH)]
        vec_in = sem("vec_in")
        gw_in = sem("gw_in")
        lam_loaded = sem("lam_loaded")
        raw_in = [sem(f"raw_in{i}") for i in range(RAWS)]
        whi_done = sem("whi_done")
        wlo_done = sem("wlo_done")
        tile_done = sem("tile_done")
        bank_read = sem("bank_read")
        ohi_done = sem("ohi_done")
        olo_done = sem("olo_done")
        sq_done = sem("sq_done")
        acc_done = sem("acc_done")
        stats_done = sem("stats_done")
        ln_done = sem("ln_done")
        guess_done = sem("guess_done")
        rstd_done = sem("rstd_done")
        consts_done = sem("consts_done")
        xb_done = sem("xb_done")
        conv_done = sem("conv_done")
        xchi_done = sem("xchi_done")
        xclo_done = sem("xclo_done")
        gwhi_done = sem("gwhi_done")
        gwlo_done = sem("gwlo_done")
        gates_mm = sem("gates_mm")
        gates_act = sem("gates_act")
        ix_done = sem("ix_done")
        decay_done = sem("decay_done")
        sq_u_done = sem("sq_u_done")
        y_done = sem("y_done")
        ysq_done = sem("ysq_done")
        arg_done = sem("arg_done")
        tanh_done = sem("tanh_done")
        gelu_done = sem("gelu_done")
        lru_exp = sem("lru_exp")
        lru_q = sem("lru_q")
        lru_a = sem("lru_a")
        sqrt_done = sem("sqrt_done")
        bx_done = sem("bx_done")
        hs_done = sem("hs_done")
        lam_prod = sem("lam_prod")
        lam_exp = sem("lam_exp")
        kqhi_done = sem("kqhi_done")
        kqlo_done = sem("kqlo_done")
        scores_mm = sem("scores_mm")
        scores_read = sem("scores_read")
        exp_done = sem("exp_done")
        prob_done = sem("prob_done")
        trans_mm = sem("trans_mm")
        trans_read = sem("trans_read")
        value_done = sem("value_done")
        att_mm = sem("att_mm")
        att_read = sem("att_read")
        sub_mm = sem("sub_mm")
        sub_read = sem("sub_read")
        sub_guess = sem("sub_guess")
        sub_rstd = sem("sub_rstd")
        att_done = sem("att_done")
        half_mm = sem("half_mm")
        half_done = sem("half_done")
        half_sq = sem("half_sq")
        gained = sem("gained")
        out_dve = sem("out_dve")
        out_pool = sem("out_pool")
        stored = sem("stored")
        act_own = sem("act_own")
        dve_own = sem("dve_own")
        pool_own = sem("pool_own")

        def col(name, n=0):
            c = COLS[name] + n
            return vec[:, c:c + 1]

        class Own:

            def __init__(self, eng, s):
                self.eng, self.s, self.n, self.i, self.per = eng, s, 0, None, 0

            def step(self, ins):
                ins.then_inc(self.s, 1)
                self.n += 1

            def wait(self):
                self.eng.wait_ge(self.s, at(self.n, self.i, self.per))

            def enter(self, i, per):
                self.i, self.per, self.first = i, per, self.n

            def leave(self, times):
                assert self.n == self.first + self.per, (self.n, self.first, self.per)
                self.i, self.n = None, self.first + self.per * times

        block = keep.enter_context(nc.Block())

        @block.sync
        def _(sp):
            def load(t, slot):
                sp.dma_start(w_raw[:, slot, :], weights[t]).then_inc(raw_in[slot], 16)

            sp.dma_start(vec[:, :], vectors).then_inc(vec_in, 16)
            for m in range(NCH):
                sp.dma_start(x[:, m, :], x_t[m]).then_inc(x_in[m], 16)
                if m < RAWS:
                    load(m, m)
            with sp.Fori(1, TILES // RAWS) as i:
                for slot in range(RAWS):
                    sp.wait_ge(wlo_done, i * RAWS + (slot - RAWS + 1))
                    sp.dma_start(w_raw[:, slot, :],
                                 weights[bass.ds(i * RAWS + slot, 1)].rearrange("o p f -> (o p) f")
                                 ).then_inc(raw_in[slot], 16)
            for n, cs in enumerate(HALVES):
                for pair in range(0, NCH, 2):
                    for m in (pair, pair + 1):
                        if m in POOL_OUT:
                            sp.wait_ge(out_pool, n * len(POOL_OUT) + POOL_OUT.index(m) + 1)
                        else:
                            sp.wait_ge(out_dve, n * len(DVE_OUT) + DVE_OUT.index(m) + 1)
                    sp.dma_start(out_t[pair:pair + 2, :, cs].rearrange("m p s -> p m s"),
                                 att[:, pair:pair + 2, cs]).then_inc(stored, 16)
            sp.wait_ge(stored, 16 * (NCH // 2) * len(HALVES))

        @block.gpsimd
        def _(pool):
            own = Own(pool, pool_own)
            own.step(nc.gpsimd.memset(ones[:, :], 1.0))
            own.step(nc.gpsimd.memset(three_halves[:, :], 1.5))
            own.step(nc.gpsimd.memset(eps_col[:, :], NORM_EPS))
            for i in range(2):
                own.step(nc.gpsimd.memset(xb_pad[i][:, 0:PAD], 0.0))
            own.wait()
            nc.gpsimd.memset(cols[:, 0, 0:1], 0.0).then_inc(consts_done, 1)

            def accumulate(n, chunks=NCH):
                for m in range(chunks):
                    pool.wait_ge(sq_done, n * NCH + m + 1)
                    if n * NCH + m:
                        pool.wait_ge(acc_done, n * NCH + m)
                    if m == 0:
                        nc.gpsimd.tensor_copy(acc[:, :], work[:, 0, :]).then_inc(acc_done, 1)
                    else:
                        nc.gpsimd.tensor_tensor(acc[:, :], acc[:, :], work[:, m % 2, :],
                                                ALU.add).then_inc(acc_done, 1)

            def newton(v, guess, guess_sq, result, done):
                own.step(nc.gpsimd.tensor_tensor(guess_sq, guess_sq, v, ALU.mult))
                own.wait()
                n = guess_sq.shape[1]
                own.step(nc.gpsimd.tensor_tensor(guess_sq, three_halves[:, 0:n], guess_sq,
                                                 ALU.subtract))
                own.wait()
                nc.gpsimd.tensor_tensor(result, guess, guess_sq, ALU.mult).then_inc(done, 1)

            def split_lo(t, i=None, per=0):
                pool.wait_ge(whi_done, at(t + 1, i, per))
                nc.gpsimd.tensor_tensor(w_lo[:, t % RING, :], w_raw[:, t % RAWS, :],
                                        w_hi[:, t % RING, :], ALU.subtract).then_inc(wlo_done, 1)

            def gated_input(m):
                pool.wait_ge(gates_act, m + 1)
                nc.gpsimd.tensor_tensor(lru_x[:, m, :], lru_x[:, m, :], xc[m % XC],
                                        ALU.mult).then_inc(ix_done, 1)

            accumulate(N_A)
            pool.wait_ge(wlo_done, POOL_LO[0])
            pool.wait_ge(gwhi_done, 1)
            nc.gpsimd.tensor_tensor(gw_lo, gw_raw, gw_hi, ALU.subtract).then_inc(gwlo_done, 1)
            for m in range(NCH):
                split_lo(m + RING)
                if m:
                    gated_input(m - 1)
            gated_input(NCH - 1)
            for c in range(NCH):
                if c in (0, 4, 6):
                    split_lo(T_YB + RING + (0, 4, 6).index(c))
                pool.wait_ge(lru_q, c + 1)
                nc.gpsimd.tensor_scalar(lru_r[:, c, :], lru_r[:, c, :], -1.0, 1.0,
                                        ALU.mult, ALU.add).then_inc(lru_a, 1)
            split_lo(T_OUT - 1)
            for c in range(NCH):
                pool.wait_ge(sqrt_done, c + 1)
                nc.gpsimd.tensor_tensor(lru_x[:, c, :], lru_x[:, c, :], lru_v[:, c, :],
                                        ALU.mult).then_inc(bx_done, 1)
            for c in range(NCH - 1):
                pool.wait_ge(ohi_done, O_Y + c + 1)
                nc.gpsimd.tensor_tensor(u_lo[:, c, :], lru_v[:, c, :], u_hi[:, c, :],
                                        ALU.subtract).then_inc(olo_done, 1)
            accumulate(N_M0)
            own.step(nc.gpsimd.memset(ident[:, :], 0.0))
            own.step(nc.gpsimd.iota(bias[:, :], pattern=[[-1, S]], base=S - P, channel_multiplier=1,
                                    allow_small_or_imprecise_dtypes=True))
            own.wait()
            nc.gpsimd.affine_select(out=ident[:, :], in_=ident[:, :], compare_op=ALU.not_equal,
                                    fill=1.0, base=0, pattern=[[-1, P]],
                                    channel_multiplier=1).then_inc(consts_done, 1)
            own.step(nc.gpsimd.affine_select(out=bias[:, :], in_=bias[:, :], compare_op=ALU.is_ge,
                                             fill=MASKED, base=S - P, pattern=[[-1, S]],
                                             channel_multiplier=1))
            own.wait()
            nc.gpsimd.tensor_scalar(bias[:, :], bias[:, :], SLOPE_0, 0.0, ALU.mult,
                                    ALU.add).then_inc(consts_done, 1)

            accumulate(N_KV)

            def head_values(h, i, p):
                if i is not None or h >= 2:
                    pool.wait_ge(att_mm, at(h - 1, i, 2))
                src = value[:, :, h * P:(h + 1) * P] if i is None else \
                    value[:, :, bass.ds(i * (2 * P) + h * P, P)]
                nc.gpsimd.tensor_copy(value_h[:, p, :, :], src).then_inc(value_done, 1)

            def sub_newton(h, i):
                pool.wait_ge(sub_guess, at(h + 1, i, 2))
                newton(sub[:, 0, :], sub[:, 1, :], sub[:, 2, :], sub[:, 2, :], sub_rstd)

            def head_split_lo(h, i):
                t = T_QK + 2 * h + 1 + RING
                pool.wait_ge(wlo_done, at(t, i, 4))
                split_lo(t, i, 4)

            pool.wait_ge(bank_read, T_QK)
            head_values(0, None, 0)
            head_values(1, None, 1)
            head_split_lo(0, None)
            with pool.Fori(0, (HEADS - 2) // 2) as i:
                own.enter(i, 4)
                for k in range(2):
                    head_values(2 + k, i, k)
                    sub_newton(k, i)
                    head_split_lo(1 + k, i)
                own.leave((HEADS - 2) // 2)
            head_split_lo(HEADS - 1, None)
            sub_newton(HEADS - 2, None)
            accumulate(N_M1)
            accumulate(N_FINAL, NCH - 1)
            for n, cs in enumerate(HALVES):
                pool.wait_ge(rstd_done, N_FINAL + 2 + n)
                for m in POOL_OUT:
                    pool.wait_ge(gained, m + 1)
                    nc.gpsimd.tensor_tensor(att[:, m, cs], att[:, m, cs], rstd[:, cs],
                                            ALU.mult).then_inc(out_pool, 1)

        @block.scalar
        def _(act):
            own = Own(act, act_own)
            def split_hi(t, i=None, per=0):
                if i is None and t >= TILES:
                    return
                act.wait_ge(raw_in[t % RAWS], at(16 * (t // RAWS + 1), i, 16 * per // RAWS))
                if i is not None or t >= RING:
                    act.wait_ge(tile_done, at(t - RING + 1, i, per))
                nc.scalar.activation(w_hi[:, t % RING, :], w_raw[:, t % RAWS, :],
                                     ACT.Copy).then_inc(whi_done, 1)

            def operand_hi(dst, m, gain):
                nc.scalar.activation(dst[:, m, :], x[:, m, :], ACT.Copy,
                                     scale=gain).then_inc(ohi_done, 1)

            def square(n, m):
                k = n * NCH + m
                if k >= 2:
                    act.wait_ge(acc_done, k - 1)
                nc.scalar.activation(work[:, m % 2, :], x[:, m, :], ACT.Square).then_inc(sq_done, 1)

            def guess(g, psum, scale, eps, ln_done, exp_done):
                nc.scalar.activation(g, psum, ACT.Ln, scale=scale, bias=eps_col[:, eps:eps + 1]
                                     ).then_inc(ln_done[0], 1)
                act.wait_ge(*ln_done)
                nc.scalar.activation(g, g, ACT.Exp, scale=-0.5).then_inc(exp_done, 1)

            def norm_guess(n):
                act.wait_ge(stats_done, n + 1)
                k = n + (n > N_KV)
                guess(work[:, 3, :], ps[:, BANK_STATS, :], 1.0 / D, 0, (ln_done, k + 1), guess_done)
                if n == N_KV:
                    guess(cols[:, 1, :], ps[:, BANK_COLS, 0:QB], 1.0 / D, 0, (ln_done, k + 2),
                          guess_done)

            nc.scalar.preload_act_table_set("natural_log_exp_and_others")
            act.wait_ge(vec_in, 16)
            for m in range(NCH):
                act.wait_ge(x_in[m], 16)
                operand_hi(h_hi, m, col("a_norm", m))
                if m < 2:
                    split_hi(m)
                if m == 4:
                    nc.scalar.dma_start(gw_raw, gate_weights).then_inc(gw_in, 16)
                if m == NCH - 2:
                    split_hi(2)
                square(N_A, m)
            nc.scalar.dma_start(lam_in[:, :], lam_vecs).then_inc(lam_loaded, 16)
            act.wait_ge(decay_done, 1)
            nc.scalar.activation(small[:, 1, :], small[:, 0, :], ACT.Exp, scale=-1.0).then_inc(decay_done, 1)
            split_hi(3)
            act.wait_ge(consts_done, 1)
            norm_guess(N_A)
            act.wait_ge(gw_in, 16)
            nc.scalar.activation(gw_hi, gw_raw, ACT.Copy).then_inc(gwhi_done, 1)
            split_hi(RING)

            def xb_bias(m):
                act.wait_ge(bank_read, T_XB + m + 1)
                if m >= 2:
                    act.wait_ge(conv_done, m - 1)
                nc.scalar.activation(xb_pad[m % 2][:, PAD:], zr[m % 2], ACT.Identity,
                                     bias=col("b_in", m)).then_inc(xb_done, 1)

            def gate_sigmoids(m):
                act.wait_ge(gates_mm, m + 1)
                bank_r, bank_i = BANK_GATES[m % 2]
                nc.scalar.activation(lru_r[:, m, :], ps[:, bank_r, :], ACT.Sigmoid,
                                     bias=col("gate_b", m))
                nc.scalar.activation(lru_x[:, m, :], ps[:, bank_i, :], ACT.Sigmoid,
                                     bias=col("gate_b", NCH + m)).then_inc(gates_act, 1)

            xb_bias(0)
            for m in range(NCH):
                act.wait_ge(conv_done, m + 1)
                if m >= 2:
                    act.wait_ge(gates_mm, m - 1)
                nc.scalar.activation(xc_hi[m % 2], xc[m % XC], ACT.Copy).then_inc(xchi_done, 1)
                if m < NCH - 1:
                    xb_bias(m + 1)
                if m:
                    split_hi(T_XB + m + RING)
                    gate_sigmoids(m - 1)

            def gated_hi(c):
                act.wait_ge(hs_done, c + 1)
                nc.scalar.activation(u_hi[:, c, :], lru_v[:, c, :], ACT.Copy).then_inc(ohi_done, 1)

            def y_squared(m):
                act.wait_ge(bank_read, T_YB + m + 1)
                if m == 0:
                    act.wait_ge(gwlo_done, 1)
                nc.scalar.activation(gelu[:, m, :], work[:, m % 2, :], ACT.Identity,
                                     bias=col("b_in", NCH + m)).then_inc(y_done, 1)
                act.wait_ge(y_done, m + 1)
                if m >= 2:
                    act.wait_ge(gelu_done, m - 1)
                nc.scalar.activation(work[:, 2 + m % 2, :], gelu[:, m, :],
                                     ACT.Square).then_inc(ysq_done, 1)

            y_squared(0)
            for m in range(NCH):
                if m == 0:
                    gate_sigmoids(NCH - 1)
                    act.wait_ge(ix_done, NCH)
                    act.wait_ge(decay_done, 3)
                    act.wait_ge(gates_act, NCH)
                if m == 0:
                    split_hi(T_YB + RING)
                for c in DECAY_AT.get(m, ()):
                    own.step(nc.scalar.activation(lru_v[:, c, :], lru_r[:, c, :], ACT.Tanh,
                                                  scale=small[:, 8, c:c + 1]))
                    own.wait()
                    nc.scalar.activation(lru_r[:, c, :], lru_r[:, c, :], ACT.Exp,
                                         scale=small[:, 9, c:c + 1]).then_inc(lru_exp, 1)
                    if c == 3:
                        split_hi(T_YB + RING + 1)
                    if c == 5:
                        split_hi(T_YB + RING + 2)
                if 3 < m < NCH - 1:
                    for c in GATED_AT.get(m - 1, ()):
                        gated_hi(c)
                act.wait_ge(arg_done, m + 1)
                nc.scalar.activation(work[:, 2 + m % 2, :], work[:, 2 + m % 2, :], ACT.Tanh,
                                     scale=GELU_C * GELU_CUBIC).then_inc(tanh_done, 1)
                for n in Y_AT.get(m, ()):
                    y_squared(n)
                if m == SQRT_AT:
                    split_hi(T_OUT - 1)
                if m == SQRT_AT:
                    for c in range(NCH):
                        act.wait_ge(lru_q, c + 1)
                        nc.scalar.activation(lru_v[:, c, :], lru_v[:, c, :], ACT.Sqrt,
                                             scale=-1.0).then_inc(sqrt_done, 1)
                        if c == NCH // 2 - 1:
                            split_hi(T_OUT)
                for t in SPLIT_AT.get(m, ()):
                    if m == 2:
                        gated_hi(t - T_OUT - 1)
                    split_hi(t)
            gated_hi(NCH - 2)
            gated_hi(NCH - 1)
            nc.scalar.preload_act_table_set("natural_log_exp_and_others")

            def residual_step(t, n, gains, early=False):
                for m in range(NCH - (n == N_FINAL)):
                    if early:
                        split_hi(t + m + RING)
                    act.wait_ge(bank_read, t + m + 1)
                    if gains is not None:
                        operand_hi(h_hi, m, col(gains[0], gains[1] + m))
                    square(n, m)
                    if n == N_FINAL:
                        nc.scalar.activation(att[:, m, :], x[:, m, :], ACT.Copy,
                                             scale=col("final_norm", m)).then_inc(gained, 1)
                    if not early:
                        split_hi(t + m + RING)

            residual_step(T_OUT, N_M0, ("mlp_norm", 0))

            def mlp_up(t0, o0, i, norm=None):
                per = 2 * NCH
                for m in range(NCH):
                    if m == 0 and norm is not None:
                        split_hi(t0 + RING)
                        norm_guess(norm)
                    act.wait_ge(bank_read, at(t0 + m + 1, i, per))
                    nc.scalar.activation(work[:, 2 + m % 2, :], work[:, m % 2, :],
                                         ACT.Square).then_inc(sq_u_done, 1)
                    act.wait_ge(sq_u_done, at(o0 + m + 1, i, NCH))
                    nc.scalar.activation(u_hi[:, m, :], work[:, 2 + m % 2, :],
                                         ACT.Copy).then_inc(ohi_done, 1)
                    if m or norm is None:
                        split_hi(t0 + m + RING, i, per)

            def mlp(layer, t0, n_stats, n, gains):
                first_u = layer * NCH * GROUPS
                mlp_up(t0, first_u, None, n_stats)
                with act.Fori(0, GROUPS - 1) as i:
                    for m in range(NCH):
                        split_hi(t0 + NCH + m + RING, i, 2 * NCH)
                    mlp_up(t0 + 2 * NCH, first_u + NCH, i)
                residual_step(t0 + (2 * GROUPS - 1) * NCH, n, gains)

            mlp(0, T_MLP0, N_M0, N_KV, ("kv_norm", 0))

            act.wait_ge(lam_prod, 2)
            nc.scalar.activation(lam_s[:, 2:4], lam_s[:, 0:2], ACT.Exp).then_inc(lam_exp, 1)
            for m in range(NCH):
                operand_hi(u_hi, m, col("b_norm", m))
                split_hi(T_V + m + RING)
                if m == 0:
                    norm_guess(N_KV)

            def kq_split_hi(h, i, which):
                act.wait_ge(bank_read, at(T_QK + 2 * h + 2 - which, i, 4))
                nc.scalar.activation(kq_hi[:, which, :], kq[:, which, :], ACT.Copy
                                     ).then_inc(kqhi_done, 1)

            def exps(h, i, j):
                a = QB * h + j
                n = (QB - j) * P
                act.wait_ge(scores_read, at(2 * a + 2, i, 4 * QB))
                for c in range(2):
                    ins = nc.scalar.activation(prob[:, j % 2, c, 0:n], prob[:, j % 2, c, 0:n], ACT.Exp,
                                               scale=-1.0, bias=neg_min[:, j % 2, c:c + 1],
                                               accum_out=total[:, j % 2, c:c + 1])
                ins.then_inc(exp_done, 1)

            def transposed(h, i, j):
                a = QB * h + j
                qb = QB - 1 - j
                act.wait_ge(trans_mm, at(a + 1, i, 2 * QB))
                if j == 0 and (i is not None or h > 0):
                    act.wait_ge(att_mm, at(h, i, 2))
                nc.scalar.activation(
                    prob_t[:, 0:qb + 1, qb * P:(qb + 1) * P],
                    ps[:, BANK_T, 0:(qb + 1) * P].rearrange("p (b q) -> p b q", q=P),
                    ACT.Copy).then_inc(trans_read, 1)

            def att_out(h, i):
                act.wait_ge(att_mm, at(h + 1, i, 2))
                if i is not None or h > 0:
                    act.wait_ge(att_done, at(h, i, 2))
                if h == HEADS - 1:
                    nc.scalar.activation(sub[:, 0, :], ps[:, BANK_O, :], ACT.Square).then_inc(att_read, 1)
                    nc.scalar.activation(o_raw, ps[:, BANK_O, :], ACT.Copy)
                    return
                nc.scalar.activation(o_raw, ps[:, BANK_O, :], ACT.Copy)
                nc.scalar.activation(sub[:, 0, :], ps[:, BANK_O, :], ACT.Square).then_inc(att_read, 1)

            def sub_guess_of(h, i):
                act.wait_ge(sub_mm, at(h + 1, i, 2))
                bank = BANK_T if h == HEADS - 1 else BANK_O
                own.step(nc.scalar.activation(sub[:, 0, :], ps[:, bank, :], ACT.Copy,
                                              scale=0.5 / V_DIM, bias=0.5 * SUBLN_EPS))
                own.wait()
                nc.scalar.activation(sub[:, 1, :], sub[:, 0, :], ACT.Ln, scale=2.0
                                     ).then_inc(sub_read, 1)
                act.wait_ge(sub_read, at(h + 1, i, 2))
                own.step(nc.scalar.activation(sub[:, 1, :], sub[:, 1, :], ACT.Exp, scale=-0.5))
                own.wait()
                nc.scalar.activation(sub[:, 2, :], sub[:, 1, :], ACT.Square).then_inc(sub_guess, 1)

            def attended_hi(m):
                act.wait_ge(att_done, m + 1)
                nc.scalar.activation(u_hi[:, m, :], att[:, m, :], ACT.Copy).then_inc(ohi_done, 1)

            def head(h, i, first=False, last=False):
                t = T_QK + 2 * h + RING
                if last:
                    act.wait_ge(tile_done, T_O - 1)
                    for m in range(4):
                        attended_hi(m)
                if not last:
                    split_hi(t, i, 4)
                if not first:
                    att_out(h - 1, i)
                if last:
                    split_hi(t)
                exps(h, i, 0)
                exps(h, i, 1)
                if last:
                    for m in range(4, HEADS - 2):
                        attended_hi(m)
                if not first:
                    sub_guess_of(h - 1, i)
                transposed(h, i, 0)
                exps(h, i, 2)
                split_hi(t + 1, i, 4)
                transposed(h, i, 1)
                exps(h, i, 3)
                transposed(h, i, 2)
                if not last:
                    kq_split_hi(h + 1, i, 1)
                transposed(h, i, 3)
                if not last:
                    kq_split_hi(h + 1, i, 0)

            kq_split_hi(0, None, 1)
            kq_split_hi(0, None, 0)
            head(0, None, first=True)
            with act.Fori(0, (HEADS - 2) // 2) as i:
                own.enter(i, 4)
                head(1, i)
                head(2, i)
                own.leave((HEADS - 2) // 2)
            head(HEADS - 1, None, last=True)
            att_out(HEADS - 1, None)
            sub_guess_of(HEADS - 1, None)
            attended_hi(HEADS - 2)
            attended_hi(HEADS - 1)
            residual_step(T_O, N_M1, ("mlp_norm", NCH), early=True)
            mlp(1, T_MLP1, N_M1, N_FINAL, None)
            m = NCH - 1
            act.wait_ge(acc_done, N_FINAL * NCH + m - 1)
            for n, cs in enumerate(HALVES):
                act.wait_ge(half_done, n + 1)
                nc.scalar.activation(work[:, m % 2, cs], x[:, m, cs], ACT.Square).then_inc(half_sq, 1)
                act.wait_ge(stats_done, N_FINAL + 1 + n)
                guess(work[:, 3, cs], ps[:, BANK_FINAL[n], cs], 1.0 / D, 0,
                      (ln_done, N_FINAL + 2 + n), guess_done)
                nc.scalar.activation(att[:, m, cs], x[:, m, cs], ACT.Copy,
                                     scale=col("final_norm", m)).then_inc(gained, 1)

        @block.vector
        def _(dve):
            own = Own(dve, dve_own)

            def split_lo(t, i=None, per=0):
                if i is None and t >= TILES:
                    return
                dve.wait_ge(whi_done, at(t + 1, i, per))
                nc.vector.tensor_tensor(w_lo[:, t % RING, :], w_raw[:, t % RAWS, :],
                                        w_hi[:, t % RING, :], ALU.subtract).then_inc(wlo_done, 1)

            def operand_lo(dst_lo, dst_hi, m, gain, o):
                dve.wait_ge(ohi_done, o + 1)
                nc.vector.scalar_tensor_tensor(out=dst_lo[:, m, :], in0=x[:, m, :], scalar=gain,
                                               in1=dst_hi[:, m, :], op0=ALU.mult,
                                               op1=ALU.subtract).then_inc(olo_done, 1)

            dve.wait_ge(vec_in, 16)
            lam = vec[:, COLS["lambda"]:COLS["lambda"] + NCH]
            own.step(nc.vector.tensor_scalar(small[:, 7, :], lam, -1.0, None, ALU.mult))
            own.wait()
            nc.vector.tensor_tensor(small[:, 0, :], lam, small[:, 7, :], ALU.max).then_inc(decay_done, 1)
            for m in range(NCH):
                dve.wait_ge(x_in[m], 16)
                operand_lo(h_lo, h_hi, m, col("a_norm", m), O_A + m)
                if m < 2:
                    split_lo(m)
                if m == NCH - 2:
                    split_lo(2)
            split_lo(3)

            def newton(psum, v, g, tmp, result, k):
                dve.wait_ge(ln_done, k + 1)
                own.step(nc.vector.tensor_scalar(v, psum, -0.5 / D, -0.5 * NORM_EPS, ALU.mult, ALU.add))
                dve.wait_ge(guess_done, k + 1)
                own.wait()
                own.step(nc.vector.tensor_tensor(tmp, g, v, ALU.mult))
                own.wait()
                own.step(nc.vector.tensor_tensor(tmp, tmp, g, ALU.mult))
                own.wait()
                nc.vector.scalar_tensor_tensor(out=result, in0=tmp, scalar=1.5, in1=g, op0=ALU.add,
                                               op1=ALU.mult).then_inc(rstd_done, 1)
                dve.wait_ge(rstd_done, k + 1)

            def norm_newton(n):
                k = n + (n > N_KV)
                newton(ps[:, BANK_STATS, :], work[:, 2, :], work[:, 3, :], work[:, 1, :], rstd[:, :], k)
                if n == N_KV:
                    newton(ps[:, BANK_COLS, 0:QB], cols[:, 0, :], cols[:, 1, :], cols[:, 2, :],
                           rstd_col[:, :], k + 1)


            def decay():
                dve.wait_ge(decay_done, 2)
                own.step(nc.vector.tensor_scalar(small[:, 2, :], small[:, 1, :], 2.0, None, ALU.add))
                own.wait()
                own.step(nc.vector.reciprocal(small[:, 3, :], small[:, 2, :]))
                own.wait()
                own.step(nc.vector.tensor_tensor(small[:, 4, :], small[:, 1, :], small[:, 3, :], ALU.mult))
                own.wait()
                own.step(nc.vector.tensor_tensor(small[:, 5, :], small[:, 4, :], small[:, 4, :], ALU.mult))
                own.wait()
                own.step(nc.vector.tensor_scalar(small[:, 6, :], small[:, 5, :], 1.0 / 17.0, None, ALU.mult))
                own.wait()
                for k in range(15, 1, -2):
                    own.step(nc.vector.scalar_tensor_tensor(
                        out=small[:, 6, :], in0=small[:, 6, :], scalar=1.0 / k, in1=small[:, 5, :],
                        op0=ALU.add, op1=ALU.mult))
                    own.wait()
                own.step(nc.vector.scalar_tensor_tensor(
                    out=small[:, 6, :], in0=small[:, 6, :], scalar=1.0, in1=small[:, 4, :],
                    op0=ALU.add, op1=ALU.mult))
                own.step(nc.vector.tensor_scalar(small[:, 7, :], small[:, 7, :], 0.0, None, ALU.max))
                own.wait()
                own.step(nc.vector.scalar_tensor_tensor(
                    out=small[:, 7, :], in0=small[:, 6, :], scalar=2.0, in1=small[:, 7, :],
                    op0=ALU.mult, op1=ALU.add))
                own.wait()
                own.step(nc.vector.tensor_scalar(small[:, 8, :], small[:, 7, :], LRU_C / 2, None, ALU.mult))
                nc.vector.tensor_scalar(small[:, 9, :], small[:, 7, :], -LRU_C, None,
                                        ALU.mult).then_inc(decay_done, 1)

            def branch(m):
                t = T_XB + m
                dve.wait_ge(tile_done, t + 1)
                if m >= 2:
                    dve.wait_ge(xb_done, m - 1)
                nc.vector.tensor_tensor(zr[m % 2], ps[:, t % RING, :], rstd[:, :],
                                        ALU.mult).then_inc(bank_read, 1)

            norm_newton(N_A)
            branch(0)
            for m in range(NCH):
                dve.wait_ge(xb_done, m + 1)
                if m >= XC:
                    dve.wait_ge(ix_done, m - XC + 1)
                pad = xb_pad[m % 2]
                own.step(nc.vector.tensor_scalar(xc[m % XC], pad[:, PAD:PAD + S],
                                                 col("conv_w", PAD * NCH + m), col("conv_b", m),
                                                 ALU.mult, ALU.add))
                for j in range(PAD - 1, -1, -1):
                    own.wait()
                    ins = nc.vector.scalar_tensor_tensor(
                        out=xc[m % XC], in0=pad[:, j:j + S], scalar=col("conv_w", j * NCH + m),
                        in1=xc[m % XC], op0=ALU.mult, op1=ALU.add)
                    if j:
                        own.step(ins)
                    else:
                        ins.then_inc(conv_done, 1)
                if m < NCH - 1:
                    branch(m + 1)
                dve.wait_ge(xchi_done, m + 1)
                nc.vector.tensor_tensor(xc_lo[m % 2], xc[m % XC], xc_hi[m % 2],
                                        ALU.subtract).then_inc(xclo_done, 1)
                if m == 3:
                    decay()

            def gelu_gate(m):
                dve.wait_ge(tanh_done, m + 1)
                nc.vector.scalar_tensor_tensor(
                    out=gelu[:, m, :], in0=work[:, 2 + m % 2, :], scalar=1.0, in1=gelu[:, m, :],
                    op0=ALU.add, op1=ALU.mult).then_inc(gelu_done, 1)

            def recurrence(c):
                dve.wait_ge(bx_done, c + 1)
                dve.wait_ge(lru_a, c + 1)
                own.step(nc.vector.tensor_tensor_scan(
                    lru_v[:, c, :], lru_r[:, c, :], lru_x[:, c, :], 0.0, ALU.mult, ALU.add))

            def gated(c):
                own.wait()
                dve.wait_ge(gelu_done, c + 1)
                nc.vector.scalar_tensor_tensor(out=lru_v[:, c, :], in0=lru_v[:, c, :], scalar=0.5,
                                               in1=gelu[:, c, :], op0=ALU.mult,
                                               op1=ALU.mult).then_inc(hs_done, 1)

            def gelu_arg(m):
                dve.wait_ge(ysq_done, m + 1)
                nc.vector.scalar_tensor_tensor(
                    out=work[:, 2 + m % 2, :], in0=work[:, 2 + m % 2, :], scalar=1.0 / GELU_CUBIC,
                    in1=gelu[:, m, :], op0=ALU.add, op1=ALU.mult).then_inc(arg_done, 1)

            def y_scaled(m):
                t = T_YB + m
                dve.wait_ge(tile_done, t + 1)
                if m >= 2:
                    dve.wait_ge(y_done, m - 1)
                nc.vector.tensor_tensor(work[:, m % 2, :], ps[:, t % RING, :], rstd[:, :],
                                        ALU.mult).then_inc(bank_read, 1)

            y_scaled(0)
            for m in range(NCH):
                if m < NCH - 1:
                    gelu_arg(m)
                if m == NCH - 2:
                    gelu_arg(m + 1)
                for n in Y_AT.get(m, ()):
                    y_scaled(n)
                for c in DECAY_AT.get(m, ()):
                    dve.wait_ge(lru_exp, c + 1)
                    own.step(nc.vector.scalar_tensor_tensor(
                        out=lru_r[:, c, :], in0=lru_r[:, c, :], scalar=1.0, in1=lru_v[:, c, :],
                        op0=ALU.add, op1=ALU.mult))
                    own.wait()
                    nc.vector.scalar_tensor_tensor(
                        out=lru_v[:, c, :], in0=lru_r[:, c, :], scalar=-2.0, in1=lru_r[:, c, :],
                        op0=ALU.add, op1=ALU.mult).then_inc(lru_q, 1)
                for c in SCAN_AT.get(m, ()):
                    recurrence(c)
                    if c == 0:
                        dve.wait_ge(wlo_done, T_OUT)
                        split_lo(T_OUT)
                if m == 3:
                    split_lo(T_OUT + 1)
                    split_lo(T_OUT + 2)
                gelu_gate(m)
                for c in GATED_AT.get(m, ()):
                    gated(c)
            dve.wait_ge(olo_done, O_Y + NCH - 1)
            dve.wait_ge(ohi_done, O_Y + NCH)
            nc.vector.tensor_tensor(u_lo[:, NCH - 1, :], lru_v[:, NCH - 1, :], u_hi[:, NCH - 1, :],
                                    ALU.subtract).then_inc(olo_done, 1)

            def residual_step(t, o0, gains, early=False):
                for m in range(NCH - (t + NCH == TILES)):
                    dve.wait_ge(tile_done, t + m + 1)
                    nc.vector.tensor_tensor(x[:, m, :], x[:, m, :], ps[:, (t + m) % RING, :],
                                            ALU.add).then_inc(bank_read, 1)
                    if not early:
                        split_lo(t + m + RING - 1)
                    elif m < NCH - 1:
                        split_lo(t + m + RING)
                    if gains is not None:
                        operand_lo(h_lo, h_hi, m, col(gains[0], gains[1] + m), o0 + m)

            residual_step(T_OUT, O_M0, ("mlp_norm", 0))

            def mlp_up(t0, u0, o0, i, norm=None):
                per = 2 * NCH
                for m in range(NCH):
                    t = t0 + m
                    if m == 0 and norm is not None:
                        split_lo(t + RING - 1)
                        norm_newton(norm)
                    dve.wait_ge(tile_done, at(t + 1, i, per))
                    if u0 + m >= 2:
                        dve.wait_ge(sq_u_done, at(u0 + m - 1, i, NCH))
                    nc.vector.scalar_tensor_tensor(
                        out=work[:, m % 2, :], in0=ps[:, t % RING, :], scalar=0.0, in1=rstd[:, :],
                        op0=ALU.max, op1=ALU.mult).then_inc(bank_read, 1)
                    if m or norm is None:
                        split_lo(t + RING - 1, i, per)
                    dve.wait_ge(ohi_done, at(o0 + m + 1, i, NCH))
                    nc.vector.tensor_tensor(u_lo[:, m, :], work[:, 2 + m % 2, :], u_hi[:, m, :],
                                            ALU.subtract).then_inc(olo_done, 1)

            def mlp(layer, t0, n_stats, o_next, gains):
                u0 = layer * NCH * GROUPS
                o0 = O_U1 if layer else O_U0
                mlp_up(t0, u0, o0, None, n_stats)
                with dve.Fori(0, GROUPS - 1) as i:
                    for m in range(NCH):
                        t = t0 + NCH + m
                        dve.wait_ge(tile_done, at(t + 1, i, 2 * NCH))
                        nc.vector.tensor_tensor(x[:, m, :], x[:, m, :], ps[:, t % RING, :],
                                                ALU.add).then_inc(bank_read, 1)
                        split_lo(t + RING - 1, i, 2 * NCH)
                    mlp_up(t0 + 2 * NCH, u0 + NCH, o0 + NCH, i)
                residual_step(t0 + (2 * GROUPS - 1) * NCH, o_next, gains)

            mlp(0, T_MLP0, N_M0, O_KV, ("kv_norm", 0))

            dve.wait_ge(lam_loaded, 16)
            for k in range(2):
                nc.vector.tensor_tensor_reduce(
                    out=lam_tmp[:, :], in0=lam_in[:, 2 * k * HEAD_DIM:(2 * k + 1) * HEAD_DIM],
                    in1=lam_in[:, (2 * k + 1) * HEAD_DIM:(2 * k + 2) * HEAD_DIM], scale=1.0, scalar=0.0,
                    op0=ALU.mult, op1=ALU.add, accum_out=lam_s[:, k:k + 1]).then_inc(lam_prod, 1)
                dve.wait_ge(lam_prod, k + 1)
            dve.wait_ge(lam_exp, 1)
            own.step(nc.vector.tensor_tensor(lam_s[:, 4:5], lam_s[:, 3:4], lam_s[:, 2:3], ALU.subtract))
            own.wait()
            own.step(nc.vector.tensor_scalar(lam_s[:, 5:6], lam_s[:, 4:5], LAM_INIT, None, ALU.subtract))
            own.step(nc.vector.tensor_scalar(lam_s[:, 6:7], col("subln"), 1.0 - LAM_INIT, None, ALU.mult))
            own.wait()
            neg_lam, sub_gain = lam_s[:, 5:6], lam_s[:, 6:7]

            for half in range(2):
                for s in range(4):
                    m = half * 4 + s
                    split_lo(T_V + m + RING - 1)
                    operand_lo(u_lo, u_hi, m, col("b_norm", m), O_Q + m)
                    if m == 0:
                        norm_newton(N_KV)
                dve.wait_ge(tile_done, T_V + 4 * half + 4)
                for tok in range(QB):
                    nc.vector.tensor_scalar(value[:, tok, half * S:(half + 1) * S],
                                            ps[:, 4 * half + tok, :], rstd_col[:, tok:tok + 1], None,
                                            ALU.mult).then_inc(bank_read, 1)

            def key(h, i):
                t = T_QK + 2 * h + 1
                dve.wait_ge(tile_done, at(t + 1, i, 4))
                nc.vector.tensor_tensor(kq[:, 0, :], ps[:, 0, :], rstd[:, :],
                                        ALU.mult).then_inc(bank_read, 1)

            def query(h, i):
                t = T_QK + 2 * h
                dve.wait_ge(tile_done, at(t + 1, i, 4))
                nc.vector.scalar_tensor_tensor(out=kq[:, 1, :], in0=ps[:, 1, :],
                                               scalar=-HEAD_DIM ** -0.5, in1=rstd[:, :], op0=ALU.mult,
                                               op1=ALU.mult).then_inc(bank_read, 1)

            def kq_split_lo(h, i, which):
                dve.wait_ge(kqhi_done, at(2 * h + 2 - which, i, 4))
                nc.vector.tensor_tensor(kq_lo[:, which, :], kq[:, which, :], kq_hi[:, which, :],
                                        ALU.subtract).then_inc(kqlo_done, 1)

            def biased(h, i, j):
                a = QB * h + j
                n = (QB - j) * P
                dve.wait_ge(scores_mm, at(a + 1, i, 2 * QB))
                if i is not None or a >= 2:
                    dve.wait_ge(trans_mm, at(a - 1, i, 2 * QB))
                nc.vector.memset(absorb[:, j % 2:j % 2 + 1], 0.0)
                for c in range(2):
                    nc.vector.tensor_tensor_reduce(
                        out=prob[:, j % 2, c, 0:n], in0=ps[:, BANK_SCORES + 2 * (j % 2) + c, 0:n],
                        in1=bias[:, S - n:S], scale=1.0, scalar=MASKED, op0=ALU.add, op1=ALU.min,
                        accum_out=neg_min[:, j % 2, c:c + 1]).then_inc(scores_read, 1)

            def combined(h, i, j):
                a = QB * h + j
                n = (QB - j) * P
                s = j % 2
                dve.wait_ge(exp_done, at(a + 1, i, 2 * QB))
                own.step(nc.vector.reciprocal(inv[:, s, :], total[:, s, :]))
                own.wait()
                own.step(nc.vector.tensor_tensor(inv_lam[:, s:s + 1], inv[:, s, 1:2], neg_lam, ALU.mult))
                own.wait()
                own.step(nc.vector.tensor_scalar(prob[:, s, 1, 0:n], prob[:, s, 1, 0:n],
                                                 inv_lam[:, s:s + 1], None, ALU.mult))
                own.wait()
                nc.vector.scalar_tensor_tensor(out=prob[:, s, 0, 0:n], in0=prob[:, s, 0, 0:n],
                                               scalar=inv[:, s, 0:1], in1=prob[:, s, 1, 0:n],
                                               op0=ALU.mult, op1=ALU.add).then_inc(prob_done, 1)

            def normed(h, i):
                dve.wait_ge(sub_rstd, at(h + 1, i, 2))
                dst = att[:, h, :] if i is None else \
                    att[:, bass.ds(i * 2 + h, 1), :].rearrange("p o s -> p (o s)")
                nc.vector.scalar_tensor_tensor(out=dst, in0=o_raw, scalar=sub_gain,
                                               in1=sub[:, 2, :], op0=ALU.mult,
                                               op1=ALU.mult).then_inc(att_done, 1)

            OWN_PER_HEAD = 3 * QB + 1

            def attended_lo(m):
                dve.wait_ge(ohi_done, O_ATT + m + 1)
                nc.vector.tensor_tensor(u_lo[:, m, :], att[:, m, :], u_hi[:, m, :],
                                        ALU.subtract).then_inc(olo_done, 1)

            def head_split_lo(h, i):
                t = T_QK + 2 * h + RING
                dve.wait_ge(wlo_done, at(t, i, 4))
                split_lo(t, i, 4)

            def head(h, i, first=False, last=False):
                if last:
                    for m in range(3):
                        attended_lo(m)
                else:
                    head_split_lo(h, i)
                biased(h, i, 0)
                biased(h, i, 1)
                if last:
                    attended_lo(3)
                combined(h, i, 0)
                if last:
                    for m in range(4, HEADS - 2):
                        attended_lo(m)
                combined(h, i, 1)
                if last:
                    head_split_lo(h, i)
                biased(h, i, 2)
                combined(h, i, 2)
                biased(h, i, 3)
                dve.wait_ge(scores_read, at(2 * QB * (h + 1), i, 4 * QB))
                own.step(nc.vector.tensor_scalar(bias[:, :], bias[:, :], 0.5, None, ALU.mult))
                combined(h, i, 3)
                if not last:
                    query(h + 1, i)
                if not first:
                    normed(h - 1, i)
                if not last:
                    kq_split_lo(h + 1, i, 1)
                    key(h + 1, i)
                    kq_split_lo(h + 1, i, 0)

            query(0, None)
            split_lo(T_QK + RING - 1)
            kq_split_lo(0, None, 1)
            key(0, None)
            kq_split_lo(0, None, 0)
            dve.wait_ge(consts_done, 3)
            head(0, None, first=True)
            with dve.Fori(0, (HEADS - 2) // 2) as i:
                own.enter(i, 2 * OWN_PER_HEAD)
                head(1, i)
                head(2, i)
                own.leave((HEADS - 2) // 2)
            head(HEADS - 1, None, last=True)
            attended_lo(HEADS - 2)
            dve.wait_ge(sub_guess, HEADS)
            own.step(nc.vector.tensor_tensor(sub[:, 2, :], sub[:, 2, :], sub[:, 0, :], ALU.mult))
            own.wait()
            own.step(nc.vector.tensor_scalar(sub[:, 2, :], sub[:, 2, :], -1.0, 1.5, ALU.mult, ALU.add))
            own.wait()
            nc.vector.tensor_tensor(sub[:, 2, :], sub[:, 1, :], sub[:, 2, :],
                                    ALU.mult).then_inc(sub_rstd, 1)
            normed(HEADS - 1, None)
            attended_lo(HEADS - 1)
            dve.wait_ge(wlo_done, T_O + RING)
            residual_step(T_O, O_M1, ("mlp_norm", NCH), early=True)
            mlp(1, T_MLP1, N_M1, None, None)
            for n, cs in enumerate(HALVES):
                dve.wait_ge(half_mm, n + 1)
                nc.vector.tensor_tensor(x[:, NCH - 1, cs], x[:, NCH - 1, cs], ps[:, BANK_LAST[n], cs],
                                        ALU.add).then_inc(half_done, 1)
            for n, cs in enumerate(HALVES):
                newton(ps[:, BANK_FINAL[n], cs], work[:, 2, cs], work[:, 3, cs], work[:, 1, cs],
                       rstd[:, cs], N_FINAL + 1 + n)
                for m in DVE_OUT:
                    dve.wait_ge(gained, m + 1 + (n if m == NCH - 1 else 0))
                    nc.vector.tensor_tensor(att[:, m, cs], att[:, m, cs], rstd[:, cs],
                                            ALU.mult).then_inc(out_dve, 1)

        @block.tensor
        def _(pe):
            def passes(bank, slot, hi, lo, k, parts=(0, 1, 2)):
                ws = slice(k * P, (k + 1) * P)
                pairs = ((w_hi, hi), (w_hi, lo), (w_lo, hi))
                for n in parts:
                    w, o = pairs[n]
                    ins = nc.tensor.matmul(ps[:, bank, :], w[:, slot, ws], o[:, k, :],
                                           start=(k == 0 and n == 0), stop=(k == NCH - 1 and n == 2))
                return ins

            def tile_starts(t, free, i=None, per=0):
                pe.wait_ge(wlo_done, at(t + 1, i, per))
                if i is not None or free > 0:
                    pe.wait_ge(bank_read, at(free, i, per))

            def tile(t, hi, lo, o=None, i=None, per=0, o_per=0):
                tile_starts(t, t - RING + 1, i, per)
                for k in range(NCH):
                    if o is not None:
                        pe.wait_ge(olo_done, at(o + k + 1, i, o_per))
                    ins = passes(t % RING, t % RING, hi, lo, k)
                ins.then_inc(tile_done, 1)

            def open_tiles(t0, n, hi, lo, o, lag=0):
                for step in range(NCH + lag):
                    for t in range(t0, t0 + n):
                        k = step - (lag if t == t0 + n - 1 else 0)
                        if k not in range(NCH):
                            continue
                        if k == 0:
                            tile_starts(t, t - RING + 1)
                        pe.wait_ge(olo_done, o + k + 1)
                        ins = passes(t % RING, t % RING, hi, lo, k)
                        if k == NCH - 1:
                            ins.then_inc(tile_done, 1)

            def stats(n):
                pe.wait_ge(acc_done, (n + 1) * NCH)
                ins = nc.tensor.matmul(ps[:, BANK_STATS, :], ones[:, :], acc[:, :], start=True,
                                       stop=True)
                if n == N_KV:
                    for tok in range(QB):
                        ins = nc.tensor.matmul(ps[:, BANK_COLS, tok:tok + 1],
                                               acc[:, tok * P:(tok + 1) * P], ones[:, 0:1],
                                               start=True, stop=True)
                ins.then_inc(stats_done, 1)

            def gates(m):
                pe.wait_ge(xclo_done, m + 1)
                if m == 0:
                    pe.wait_ge(gwlo_done, 1)
                if m == 1:
                    pe.wait_ge(rstd_done, N_A + 1)
                if m >= 2:
                    pe.wait_ge(gates_act, m - 1)
                for g, bank in enumerate(BANK_GATES[m % 2]):
                    ws = slice((g * NCH + m) * P, (g * NCH + m + 1) * P)
                    for n, (w, o) in enumerate(((gw_hi, xc_hi), (gw_hi, xc_lo), (gw_lo, xc_hi))):
                        ins = nc.tensor.matmul(ps[:, bank, :], w[:, ws], o[m % 2],
                                               start=(n == 0), stop=(n == 2))
                ins.then_inc(gates_mm, 1)

            pe.wait_ge(consts_done, 1)
            for _ in range(WARM_UP):
                nc.tensor.matmul(ps[:, BANK_STATS, :], ones[:, :], three_halves[:, :], start=True,
                                 stop=True)
            open_tiles(T_XB, 2, h_hi, h_lo, O_A)
            stats(N_A)
            gates_after = {3: (0,), 4: (1,), 5: (2, 3), 6: (4,), 7: (5,), 8: (6, 7)}
            for t in range(T_XB + 2, T_OUT):
                tile(t, h_hi, h_lo)
                for m in gates_after.get(t, ()):
                    gates(m)
            open_tiles(T_OUT, OPEN, u_hi, u_lo, O_Y, lag=1)
            for m in range(OPEN, NCH):
                tile(T_OUT + m, u_hi, u_lo)

            def mlp(t0, o_h, o_u, n):
                per = 2 * NCH
                for m in range(NCH):
                    tile(t0 + m, h_hi, h_lo, o_h if m == 0 else None)
                    if m == 0:
                        stats(n)

                def down(first_t, first_o, i, last=False):
                    for m in range(NCH - last):
                        tile(first_t + m, u_hi, u_lo, first_o if m == 0 else None, i, per, NCH)

                with pe.Fori(0, GROUPS - 1) as i:
                    down(t0 + NCH, o_u, i)
                    for m in range(NCH):
                        tile(t0 + per + m, h_hi, h_lo, None, i, per)
                down(t0 + per * GROUPS - NCH, o_u + (GROUPS - 1) * NCH, None, last=n == N_M1)

            mlp(T_MLP0, O_M0, O_U0, N_M0)

            for half in range(2):
                for s in range(4):
                    t = T_V + half * 4 + s
                    tile_starts(t, T_V - 1)
                    if half == 1 and s == 0:
                        pe.wait_ge(rstd_done, N_KV + 2)
                    for kk in range(2):
                        k = 2 * s + kk
                        if half == 0:
                            pe.wait_ge(olo_done, O_KV + k + 1)
                        cs = slice(kk * S, (kk + 1) * S)
                        for tok in range(QB):
                            ts = slice(tok * P, (tok + 1) * P)
                            if half == 0 and k == 0 and tok == QB - 1:
                                pe.wait_ge(bank_read, T_V)
                            for n, (o, w) in enumerate(((h_hi, w_hi), (h_lo, w_hi), (h_hi, w_lo))):
                                ins = nc.tensor.matmul(ps[:, 4 * half + tok, :], o[:, k, ts], w[:, t % RING, cs],
                                                       start=(k == 0 and n == 0),
                                                       stop=(k == NCH - 1 and n == 2))
                    ins.then_inc(tile_done, 1)
                    if half == 0 and s == 0:
                        stats(N_KV)

            def kq_part(h, i, part):
                which, quarter = divmod(part, 4)
                t = T_QK + 2 * h + which
                if quarter == 0:
                    tile_starts(t, t - 1 if h else T_V + 4, i, 4)
                for k in (2 * quarter, 2 * quarter + 1):
                    if which == 0:
                        ins = passes(1, t % RING, u_hi, u_lo, k)
                    else:
                        ins = passes(0, t % RING, h_hi, h_lo, k)
                if quarter == 3:
                    ins.then_inc(tile_done, 1)

            def scores(h, i, j):
                a = QB * h + j
                qb = QB - 1 - j
                n = (qb + 1) * P
                if j == 0:
                    pe.wait_ge(kqlo_done, at(2 * h + 2, i, 4))
                if i is not None or a >= 2:
                    pe.wait_ge(scores_read, at(2 * (a - 1), i, 4 * QB))
                products = ((kq_hi, kq_hi), (kq_hi, kq_lo), (kq_lo, kq_hi))
                if n == P:
                    products = ((kq, kq),)
                for m, (q, k) in enumerate(products):
                    for c in range(2):
                        rows = slice(c * HEAD_DIM, (c + 1) * HEAD_DIM)
                        ins = nc.tensor.matmul(ps[:, BANK_SCORES + 2 * (j % 2) + c, 0:n],
                                               q[rows, 1, qb * P:(qb + 1) * P], k[rows, 0, 0:n],
                                               start=(m == 0), stop=(m == len(products) - 1))
                ins.then_inc(scores_mm, 1)

            def transposes(h, i, j):
                a = QB * h + j
                qb = QB - 1 - j
                pe.wait_ge(prob_done, at(a + 1, i, 2 * QB))
                if i is not None or a >= 1:
                    pe.wait_ge(trans_read, at(a, i, 2 * QB))
                for kb in range(qb + 1):
                    ks = slice(kb * P, (kb + 1) * P)
                    ins = nc.tensor.transpose(ps[:, BANK_T, ks], prob[:, j % 2, 0, ks], ident[:, :])
                ins.then_inc(trans_mm, 1)

            def attend(h, i):
                pe.wait_ge(trans_read, at(QB * (h + 1) - 1, i, 2 * QB))
                pe.wait_ge(value_done, at(h + 1, i, 2))
                if i is not None or h > 0:
                    pe.wait_ge(sub_read, at(h, i, 2))
                for kb in (1, 2, 3, 0):
                    if kb == 0:
                        pe.wait_ge(trans_read, at(QB * (h + 1), i, 2 * QB))
                    ins = nc.tensor.matmul(ps[:, BANK_O, kb * P:S], value_h[:, h % 2, kb, :],
                                           prob_t[:, kb, kb * P:S], start=(kb == 1),
                                           stop=(kb == 0), skip_group_check=True)
                ins.then_inc(att_mm, 1)

            def sub_sum(h, i):
                pe.wait_ge(att_read, at(h + 1, i, 2))
                bank = BANK_T if h == HEADS - 1 else BANK_O
                nc.tensor.matmul(ps[:, bank, :], ones[:, :], sub[:, 0, :], start=True,
                                 stop=True).then_inc(sub_mm, 1)

            def output_part(t, chunks):
                for k in chunks:
                    if k == 0:
                        tile_starts(t, T_O)
                        if t >= T_O + BANK_SCORES:
                            pe.wait_ge(scores_read, 2 * (QB * HEADS - 1))
                    pe.wait_ge(olo_done, O_ATT + k + 1)
                    passes(t % RING, t % RING, u_hi, u_lo, k)

            def head(h, i, first=False, last=False):
                def part(n):
                    if not last:
                        kq_part(h + 1, i, n)
                    else:
                        output_part(*LAST_HEAD[n])

                if not last:
                    part(0)
                scores(h, i, 0)
                scores(h, i, 1)
                if not first:
                    sub_sum(h - 1, i)
                if last:
                    part(0)
                part(1)
                scores(h, i, 2)
                part(2)
                transposes(h, i, 0)
                part(3)
                scores(h, i, 3)
                part(4)
                transposes(h, i, 1)
                part(5)
                transposes(h, i, 2)
                part(6)
                part(7)
                transposes(h, i, 3)
                attend(h, i)

            pe.wait_ge(olo_done, O_Q + NCH)
            for part in range(8):
                kq_part(0, None, part)
            pe.wait_ge(bank_read, T_QK)
            pe.wait_ge(consts_done, 3)
            head(0, None, first=True)
            with pe.Fori(0, (HEADS - 2) // 2) as i:
                head(1, i)
                head(2, i)
            head(HEADS - 1, None, last=True)
            output_part(T_O + 3, (0,))
            sub_sum(HEADS - 1, None)
            output_part(T_O + 3, (1, 2, 3, 4, 5))
            for t in range(T_O, T_O + OPEN_ATT):
                output_part(t, (HEADS - 2,))
            pe.wait_ge(olo_done, O_ATT + HEADS)
            for t in range(T_O, T_O + OPEN_ATT):
                passes(t % RING, t % RING, u_hi, u_lo, HEADS - 1).then_inc(tile_done, 1)
            for m in range(OPEN_ATT, NCH):
                tile(T_O + m, u_hi, u_lo)
            mlp(T_MLP1, O_M1, O_U1, N_M1)

            def half_passes(n, ks):
                slot = (TILES - 1) % RING
                for k in ks:
                    ws = slice(k * P, (k + 1) * P)
                    for w, o in ((w_hi, u_hi), (w_hi, u_lo), (w_lo, u_hi)):
                        ins = nc.tensor.matmul(ps[:, BANK_LAST[n], HALVES[n]], w[:, slot, ws],
                                               o[:, k, HALVES[n]], start=(k == 0 and w is w_hi and o is u_hi),
                                               stop=(k == NCH - 1 and w is w_lo))
                if ks[-1] == NCH - 1:
                    ins.then_inc(half_mm, 1)

            def half_stats(n, last):
                src = work[:, (NCH - 1) % 2, HALVES[n]] if last else acc[:, HALVES[n]]
                ins = nc.tensor.matmul(ps[:, BANK_FINAL[n], HALVES[n]], ones[:, :], src,
                                       start=not last, stop=last)
                if last:
                    ins.then_inc(stats_done, 1)

            pe.wait_ge(wlo_done, TILES)
            half_passes(0, range(NCH))
            half_passes(1, range(NCH // 2))
            pe.wait_ge(acc_done, (N_FINAL + 1) * NCH - 1)
            half_stats(0, False)
            pe.wait_ge(half_sq, 1)
            half_stats(0, True)
            half_passes(1, range(NCH // 2, NCH))
            half_stats(1, False)
            pe.wait_ge(half_sq, 2)
            half_stats(1, True)


def kernel(**inputs):
    import concourse.bacc as bacc
    from concourse.bass_utils import run_bass_kernel_spmd

    a = {k: np.asarray(v) for k, v in inputs.items()}

    def by_output(w):
        n = w.shape[1] // P
        return w.reshape(NCH, P, n, P).transpose(2, 1, 0, 3).reshape(n, P, TILE)

    def by_input(w):
        return w.reshape(4, 2, P, S).transpose(0, 2, 1, 3).reshape(4, P, TILE)

    def mlp(layer):
        for g in range(GROUPS):
            yield by_output(a["mlp_w1"][layer][:, g * D:(g + 1) * D])
            yield by_output(a["mlp_w2"][layer][g * D:(g + 1) * D])

    keys, queries = by_output(a["w_kv"][:, :D]), by_output(a["b_w_q"][0])
    parts = [by_output(a["a_w_in"][0]), by_output(a["a_w_out"][0]), *mlp(0)]
    parts += [by_input(a["w_kv"][:, D + h * S:D + (h + 1) * S]) for h in range(2)]
    parts += [np.stack([queries, keys], axis=1).reshape(2 * HEADS, P, TILE)]
    parts += [by_output(a["b_w_o"][0]), *mlp(1)]
    weights = np.ascontiguousarray(np.concatenate(parts))

    def columns(v):
        return np.asarray(v).reshape(-1, P).T

    vectors = np.ascontiguousarray(np.concatenate([columns(a[n]) for n in (
        "a_norm", "a_b_in", "a_conv_w", "a_conv_b", "a_gate_b", "a_lambda", "kv_norm", "b_norm",
        "mlp_norm", "final_norm", "b_subln")], axis=1))
    arrays = {
        "x_t": np.ascontiguousarray(a["x"][0].T).reshape(NCH, P, S),
        "weights": weights,
        "gate_weights": np.ascontiguousarray(
            a["a_gate_w"][0].transpose(2, 0, 1, 3).reshape(P, 2 * NCH * P)),
        "vectors": vectors,
        "lam_vecs": np.ascontiguousarray(np.broadcast_to(a["b_lam"].reshape(1, -1), (P, 4 * HEAD_DIM))),
    }
    nc = bacc.Bacc("TRN2", target_bir_lowering=False, num_devices=1)
    f32 = mybir.dt.float32
    args = [nc.dram_tensor(n, v.shape, f32, kind="ExternalInput").ap() for n, v in arrays.items()]
    out = nc.dram_tensor("y_t", [NCH, P, S], f32, kind="ExternalOutput").ap()
    build(nc, *args, out)
    r = run_bass_kernel_spmd(nc, [arrays], core_ids=[0])
    y = r.results[0]["y_t"].reshape(D, S).T
    return np.ascontiguousarray(y).reshape(1, S, D)
```
